# Optimizing a Trainium2 kernel written in Bass

```python
import jax, jax.numpy as jnp
from jax import lax
import numpy as np

D_MODEL = 1024
BATCH = 1
SEQ = 512
DEPTH = 2

A_WIDTH = 512
A_GROUPS = 8
A_CHUNK = 128
B_HEADS = 8
B_NOPE = 64
B_ROPE = 32
B_VDIM = 64
B_QK = B_NOPE + B_ROPE
B_Q_LORA = 384
B_KV_LORA = 256
Q_BLOCK = 128
ROPE_BASE = 10000.0
C_HEADS = 8
C_DK = 64
C_DV = 64
C_CONV = 4
C_CHUNK = 64
C_QKV = C_HEADS * (2 * C_DK + C_DV)
C_Z = C_HEADS * C_DV
N_BRANCH = 3
BRANCH_WIDTH = 512
D_FF = 4 * D_MODEL
EPS = 1e-6
SPLIT_SIZES = (A_WIDTH, A_WIDTH, B_Q_LORA, B_KV_LORA, B_ROPE, C_QKV, C_Z, C_HEADS, C_HEADS, N_BRANCH * D_MODEL)
D_IN = 2 * A_WIDTH + B_Q_LORA + B_KV_LORA + B_ROPE + C_QKV + C_Z + 2 * C_HEADS + N_BRANCH * D_MODEL

kernel_name = "hybrid_gated_gmlp_mla_deltanet"

def rms_norm(x, g):
    xf = x.astype(jnp.float32)
    y = xf * lax.rsqrt(jnp.mean(xf * xf, axis=-1, keepdims=True) + EPS)
    return (y * g.astype(jnp.float32)).astype(x.dtype)

def l2_normalize(x):
    xf = x.astype(jnp.float32)
    return xf * lax.rsqrt(jnp.sum(xf * xf, axis=-1, keepdims=True) + EPS)

def rope_tables(positions):
    half = B_ROPE // 2
    inv_freq = 1.0 / (ROPE_BASE ** (jnp.arange(half, dtype=jnp.float32) / half))
    ang = positions.astype(jnp.float32)[..., None] * inv_freq
    return jnp.cos(ang)[:, :, None, :], jnp.sin(ang)[:, :, None, :]

def rope_tail(x, cos, sin):
    half = B_ROPE // 2
    x_pass = x[..., :B_NOPE]
    x1 = x[..., B_NOPE:B_NOPE + half].astype(jnp.float32)
    x2 = x[..., B_NOPE + half:].astype(jnp.float32)
    rot = jnp.concatenate([x1 * cos - x2 * sin, x1 * sin + x2 * cos], axis=-1)
    return jnp.concatenate([x_pass, rot.astype(x.dtype)], axis=-1)

def spatial_gating_branch(a_u, a_v, sgu_norm_g, w_s, b_s):
    b, s, _ = a_u.shape
    n = s // A_CHUNK
    u = jax.nn.gelu(a_u, approximate=False)
    v = rms_norm(jax.nn.gelu(a_v, approximate=False), sgu_norm_g)
    vg = v.reshape(b, n, A_CHUNK, A_GROUPS, A_WIDTH // A_GROUPS)
    tril = jnp.tril(jnp.ones((A_CHUNK, A_CHUNK), dtype=bool))
    w = jnp.where(tril[None], w_s, jnp.zeros_like(w_s))
    sv = jnp.einsum('gts,bnsgc->bntgc', w, vg) + b_s.T[:, :, None]
    return u * sv.reshape(b, s, A_WIDTH)

def causal_block_attention(q, k, v):
    b, s, h, dq = q.shape
    nb = s // Q_BLOCK
    qb = q.reshape(b, nb, Q_BLOCK, h, dq).transpose(1, 0, 2, 3, 4)
    key_pos = jnp.arange(s)
    scale = dq ** -0.5

    def one_block(args):
        q_blk, i = args
        q_pos = i * Q_BLOCK + jnp.arange(Q_BLOCK)
        sc = jnp.einsum('bqhd,bkhd->bhqk', q_blk, k, preferred_element_type=jnp.float32) * scale
        sc = jnp.where(key_pos[None, :] <= q_pos[:, None], sc, -jnp.inf)
        p = jax.nn.softmax(sc, axis=-1)
        return jnp.einsum('bhqk,bkhv->bqhv', p.astype(v.dtype), v)

    out = lax.map(one_block, (qb, jnp.arange(nb)))
    return out.transpose(1, 0, 2, 3, 4).reshape(b, s, h, v.shape[-1])

def mla_branch(q_lat, kv_lat, k_rope, cos, sin, q_lat_norm_g, w_q_up, kv_lat_norm_g, w_kv_up, q_norm_g, k_norm_g):
    b, s, _ = q_lat.shape
    q = (rms_norm(q_lat, q_lat_norm_g) @ w_q_up).reshape(b, s, B_HEADS, B_QK)
    kv = (rms_norm(kv_lat, kv_lat_norm_g) @ w_kv_up).reshape(b, s, B_HEADS, B_NOPE + B_VDIM)
    k_nope, v = kv[..., :B_NOPE], kv[..., B_NOPE:]
    k = jnp.concatenate([k_nope, jnp.broadcast_to(k_rope[:, :, None, :], (b, s, B_HEADS, B_ROPE))], axis=-1)
    q = rope_tail(rms_norm(q, q_norm_g), cos, sin)
    k = rope_tail(rms_norm(k, k_norm_g), cos, sin)
    o = causal_block_attention(q, k, v)
    return o.reshape(b, s, B_HEADS * B_VDIM)

def causal_depthwise_conv(x, w):
    c = x.shape[-1]
    return lax.conv_general_dilated(x, w[:, None, :].astype(x.dtype), window_strides=(1,),
                                    padding=[(C_CONV - 1, 0)], dimension_numbers=('NWC', 'WIO', 'NWC'),
                                    feature_group_count=c)

def chunked_gated_delta_rule(q, k, v, g, beta):
    b, s, h, dk = q.shape
    dv = v.shape[-1]
    n = s // C_CHUNK
    q = q * (dk ** -0.5)

    def chunk(x):
        return x.reshape(b, n, C_CHUNK, h, -1).transpose(0, 3, 1, 2, 4)

    qc, kc, vc = chunk(q), chunk(k), chunk(v)
    gc = jnp.cumsum(g.reshape(b, n, C_CHUNK, h).transpose(0, 3, 1, 2), axis=-1)
    bc = beta.reshape(b, n, C_CHUNK, h).transpose(0, 3, 1, 2)
    tril = jnp.tril(jnp.ones((C_CHUNK, C_CHUNK), dtype=bool))
    strict = jnp.tril(jnp.ones((C_CHUNK, C_CHUNK), dtype=bool), -1)
    diff = gc[..., :, None] - gc[..., None, :]
    decay = jnp.exp(jnp.where(tril, diff, -jnp.inf))
    k_beta = kc * bc[..., None]
    v_beta = vc * bc[..., None]
    lower = jnp.where(strict, jnp.einsum('bhncd,bhnsd->bhncs', k_beta, kc) * decay, 0.0)
    a_mat = lower + jnp.eye(C_CHUNK, dtype=lower.dtype)
    rhs = jnp.concatenate([v_beta, k_beta * jnp.exp(gc)[..., None]], axis=-1)
    sol = lax.linalg.triangular_solve(a_mat, rhs, left_side=True, lower=True, unit_diagonal=True)
    u, w = sol[..., :dv], sol[..., dv:]
    intra = jnp.where(tril, jnp.einsum('bhncd,bhnsd->bhncs', qc, kc) * decay, 0.0)

    xs = tuple(jnp.moveaxis(t, 2, 0) for t in (qc, kc, u, w, intra, gc))

    def step(state, inp):
        q_i, k_i, u_i, w_i, a_i, g_i = inp
        v_new = u_i - jnp.einsum('bhck,bhkv->bhcv', w_i, state)
        o = (jnp.einsum('bhck,bhkv->bhcv', q_i * jnp.exp(g_i)[..., None], state)
             + jnp.einsum('bhcs,bhsv->bhcv', a_i, v_new))
        g_last = g_i[..., -1]
        state = (state * jnp.exp(g_last)[..., None, None]
                 + jnp.einsum('bhck,bhcv->bhkv', k_i * jnp.exp(g_last[..., None] - g_i)[..., None], v_new))
        return state, o

    state0 = jnp.zeros((b, h, dk, dv), dtype=jnp.float32)
    _, o = lax.scan(step, state0, xs)
    return o.transpose(1, 0, 3, 2, 4).reshape(b, s, h, dv)

def gated_deltanet_branch(c_qkv, c_z, c_b, c_a, conv_w, a_log, dt_bias, o_norm_g):
    b, s, _ = c_qkv.shape
    qkv = jax.nn.silu(causal_depthwise_conv(c_qkv, conv_w))
    q, k, v = jnp.split(qkv, [C_HEADS * C_DK, 2 * C_HEADS * C_DK], axis=-1)
    q = l2_normalize(q.reshape(b, s, C_HEADS, C_DK))
    k = l2_normalize(k.reshape(b, s, C_HEADS, C_DK))
    v = v.reshape(b, s, C_HEADS, C_DV).astype(jnp.float32)
    beta = jax.nn.sigmoid(c_b.astype(jnp.float32))
    g = -jnp.exp(a_log.astype(jnp.float32)) * jax.nn.softplus(c_a.astype(jnp.float32) + dt_bias.astype(jnp.float32))
    o = chunked_gated_delta_rule(q, k, v, g, beta)
    o = rms_norm(o, o_norm_g) * jax.nn.silu(c_z.reshape(b, s, C_HEADS, C_DV).astype(jnp.float32))
    return o.reshape(b, s, C_HEADS * C_DV).astype(c_qkv.dtype)

def setup_inputs(seed: int = 0) -> dict:
    key = jax.random.key(seed)
    ks = jax.random.split(key, 24)
    f32 = jnp.float32

    def nrm(k, shape, scale):
        return jax.random.normal(k, shape, f32) * scale

    def gain(k, shape):
        return 1.0 + 0.02 * jax.random.normal(k, shape, f32)

    x = jax.random.normal(ks[0], (BATCH, SEQ, D_MODEL), f32)
    offset = jax.random.randint(ks[1], (BATCH, 1), 0, 4096, dtype=jnp.int32)
    positions = offset + jnp.arange(SEQ, dtype=jnp.int32)[None, :]
    dt = jnp.exp(jax.random.uniform(ks[15], (DEPTH, C_HEADS), f32) * (jnp.log(0.1) - jnp.log(0.001)) + jnp.log(0.001))
    return {
        "x": x,
        "positions": positions,
        "norm1_g": gain(ks[2], (DEPTH, D_MODEL)),
        "w_in": nrm(ks[3], (DEPTH, D_MODEL, D_IN), D_MODEL ** -0.5),
        "sgu_norm_g": gain(ks[4], (DEPTH, A_WIDTH)),
        "w_spatial": nrm(ks[5], (DEPTH, A_GROUPS, A_CHUNK, A_CHUNK), A_CHUNK ** -0.5),
        "b_spatial": gain(ks[6], (DEPTH, A_GROUPS, A_CHUNK)),
        "q_lat_norm_g": gain(ks[7], (DEPTH, B_Q_LORA)),
        "w_q_up": nrm(ks[8], (DEPTH, B_Q_LORA, B_HEADS * B_QK), B_Q_LORA ** -0.5),
        "kv_lat_norm_g": gain(ks[9], (DEPTH, B_KV_LORA)),
        "w_kv_up": nrm(ks[10], (DEPTH, B_KV_LORA, B_HEADS * (B_NOPE + B_VDIM)), B_KV_LORA ** -0.5),
        "q_norm_g": gain(ks[11], (DEPTH, B_QK)),
        "k_norm_g": gain(ks[12], (DEPTH, B_QK)),
        "conv_w": nrm(ks[13], (DEPTH, C_CONV, C_QKV), C_CONV ** -0.5),
        "a_log": jnp.log(jax.random.uniform(ks[14], (DEPTH, C_HEADS), f32, 1.0, 16.0)),
        "dt_bias": dt + jnp.log(-jnp.expm1(-dt)),
        "o_norm_g": gain(ks[16], (DEPTH, C_DV)),
        "w_branch": nrm(ks[17], (DEPTH, N_BRANCH, BRANCH_WIDTH, D_MODEL), BRANCH_WIDTH ** -0.5),
        "w_out": nrm(ks[18], (DEPTH, D_MODEL, D_MODEL), D_MODEL ** -0.5),
        "norm2_g": gain(ks[19], (DEPTH, D_MODEL)),
        "w_ff1": nrm(ks[20], (DEPTH, D_MODEL, D_FF), D_MODEL ** -0.5),
        "w_ff2": nrm(ks[21], (DEPTH, D_FF, D_MODEL), D_FF ** -0.5),
    }

def reference(x, positions, norm1_g, w_in, sgu_norm_g, w_spatial, b_spatial, q_lat_norm_g, w_q_up,
              kv_lat_norm_g, w_kv_up, q_norm_g, k_norm_g, conv_w, a_log, dt_bias, o_norm_g,
              w_branch, w_out, norm2_g, w_ff1, w_ff2):
    b, s, d = x.shape
    cos, sin = rope_tables(positions)
    split_points = [int(c) for c in np.cumsum(SPLIT_SIZES)[:-1]]
    for l in range(DEPTH):
        h = rms_norm(x, norm1_g[l])
        proj = h @ w_in[l]
        a_u, a_v, q_lat, kv_lat, k_rope, c_qkv, c_z, c_b, c_a, gates = jnp.split(proj, split_points, axis=-1)
        y_a = spatial_gating_branch(a_u, a_v, sgu_norm_g[l], w_spatial[l], b_spatial[l])
        y_b = mla_branch(q_lat, kv_lat, k_rope, cos, sin, q_lat_norm_g[l], w_q_up[l],
                         kv_lat_norm_g[l], w_kv_up[l], q_norm_g[l], k_norm_g[l])
        y_c = gated_deltanet_branch(c_qkv, c_z, c_b, c_a, conv_w[l], a_log[l], dt_bias[l], o_norm_g[l])
        branches = jnp.stack([y_a, y_b, y_c], axis=2)
        y = jnp.einsum('bsnc,ncd->bsnd', branches, w_branch[l])
        gate = jax.nn.sigmoid(gates.reshape(b, s, N_BRANCH, d))
        merged = jnp.einsum('bsnd,bsnd->bsd', gate, y)
        x = x + merged @ w_out[l]
        h2 = rms_norm(x, norm2_g[l])
        x = x + jnp.square(jax.nn.relu(h2 @ w_ff1[l])) @ w_ff2[l]
    return x


_drawn_inputs = setup_inputs


def setup_inputs(seed=0):
    import zlib

    import numpy as np

    out = dict(_drawn_inputs(seed))
    spreads = {}
    factors = {'norm1_g': 2.69,
     'sgu_norm_g': 8.0,
     'b_spatial': 6.48,
     'q_lat_norm_g': 8.0,
     'kv_lat_norm_g': 8.0,
     'q_norm_g': 8.0,
     'k_norm_g': 8.0,
     'o_norm_g': 6.561}
    for name, (base, spread) in spreads.items():
        noise = np.random.default_rng([zlib.crc32(name.encode()), seed]).standard_normal(out[name].shape)
        drawn = base * np.exp(spread * noise) if base else spread * noise
        out[name] = __import__('jax').numpy.asarray(drawn.astype(out[name].dtype))
    for name, factor in factors.items():
        out[name] = (out[name] * factor).astype(out[name].dtype)
    return out
```

```python
from contextlib import ExitStack

import numpy as np

import concourse.bass as bass
from concourse import mybir

F32 = mybir.dt.float32
F32R = mybir.dt.float32r
I32 = mybir.dt.int32
ALU = mybir.AluOpType
ACT = mybir.ActivationFunctionType
AX = mybir.AxisListType

P = 128
DEPTH = 2
SEQ = 512
D = 1024
TT = SEQ // P
KD = D // P
A_WIDTH, A_GROUPS = 512, 8
HEADS = 8
PAIRS = HEADS // 2
NOPE, ROPE, VDIM = 64, 32, 64
QK = NOPE + ROPE
Q_LORA, KV_LORA = 384, 256
CHUNK, CDIM = 64, 64
CHUNKS = SEQ // CHUNK
CONV = 4
FF = 4 * D
EPS = 1e-6
ROPE_BASE = 10000.0
NEG = -1.0e30

A_U, A_V = 0, 512
Q_LAT = 1024
KV_LAT = Q_LAT + Q_LORA
K_ROPE = KV_LAT + KV_LORA
C_Q = K_ROPE + ROPE
C_K, C_V = C_Q + 512, C_Q + 1024
C_Z = C_Q + 1536
C_B = C_Z + 512
C_A = C_B + HEADS
GATES = C_A + HEADS
D_IN = GATES + 3 * D

MISC_ROPE, MISC_B, MISC_A = 0, 32, 64

TILES = (
    [("misc", 0)]
    + [("k", j) for j in range(4)] + [("q", j) for j in range(4)] + [("v", j) for j in range(4)]
    + [("z", j) for j in range(4)] + [("gate2", d) for d in range(KD)]
    + [("lat", j) for j in range(5)] + [("gate1", d) for d in range(KD)]
    + [("av", j) for j in range(4)] + [("au", j) for j in range(4)] + [("gate0", d) for d in range(KD)]
)
TILE_NO = {t: n for n, t in enumerate(TILES)}


def unit_order():
    order = []
    for t in TILES:
        if t[0] == "gate1" and t[1] == 0:
            order += [("qup", c) for c in range(4)] + [("kvup", c) for c in range(2)]
        if t[0][:4] == "gate" and t[1] % 2 == 0:
            order.append(("y" + t[0][4], t[1] // 2))
        order.append(t)
    order += [("out", n) for n in range(8)]
    for q in range(4):
        order += [("ff1", 8 * q + n) for n in range(8)] + [("ff2", 8 * q + n) for n in range(8)]
    return order


UNITS = unit_order()
UNIT_NO = {u: n for n, u in enumerate(UNITS)}
U = len(UNITS)
UCOLS = 1024
RAW, RING = 2, 4
FF0 = UNIT_NO[("ff1", 0)]
assert U % RING == 0 and FF0 % RING == 0

CST = {}
_at = 0
for _name, _n in (("ident", P), ("incl", P), ("strict", P), ("level", 6 * P), ("sel", HEADS * P), ("pair", PAIRS * P),
                  ("ind", PAIRS * 8), ("block", P), ("ones", P), ("reset", SEQ), ("causal", P), ("tril", P),
                  ("freq", ROPE // 2)):
    CST[_name] = (_at, _at + _n)
    _at += _n
NCST = _at

PRM = {}
_at = 0
for _name, _n in (("g1", KD), ("g2", KD), ("sgu", 4), ("qlat", 3), ("kvlat", 2), ("onorm", 1), ("conv", 12 * CONV),
                  ("qg", QK), ("kg", QK), ("alog", 1), ("dt", 1), ("bsp", P), ("wsp", A_GROUPS * P)):
    PRM[_name] = (_at, _at + _n)
    _at += _n
NPRM = _at

VECTOR_STEPS = 63
SCALAR_STEPS = 15

ROUND = 1.5 * 2.0 ** 23
TWO_PI = (6.28125, 8117 * 2.0 ** -22, 2 * np.pi - 6.28125 - 8117 * 2.0 ** -22)
ROPE_STEPS = 16


class Steps:

    def __init__(self):
        self.n = 0

    def next(self):
        self.n += 1
        return self.n


class PerLayer:
    unit_split = U; unit_done = U
    x_stored = 16; prm_loaded = 16; x_loaded = 16
    rstd_ready = 2; xn_ready = 8; h_turned = 16; h_hi = 16; h_lo = 16
    act_tile = 12; csq_ready = 8; csq_summed = 8
    soft_abs = 1; soft_ln = 1; soft_done = 1; cum_done = 1; ln_rows = 1; rows_done = 1; egl_done = 1; rows_turned = 1; token_done = 1
    qe_bcast = 4; qe_exp = 4; qe_done = 4
    tok_turned = 8; tok_scaled = 8; expo_done = 16; decay_done = 16; gram_done = 16; gated_done = 16
    xt_first = 4; x_turned = 8; x_first = 8; ct_ready = 20; y_done = 40; y_copied = 40; z_done = 40; z_added = 40
    solved = 8; sol_copied = 8; ws_done = 8; inter_done = 8; vnew_done = 8; supd_done = 8; state_done = 8; o_done = 4; o_copied = 4
    osq_ready = 4; osq_summed = 4; oinv_ready = 4; on_done = 4
    bval_ready = 8; b_hi = 12; b_lo = 12
    y_read = 24; m_ready = 8; m_hi = 8; m_lo = 8
    lsq_ready = 5; lsq_step = 5; linv_ready = 2; lat_val = 5; lat_hi = 5; lat_lo = 5; kr_turned = 1; kr_copied = 1; kr_placed = 1
    up_done = 10; up_copied = 16; qksq_ready = 2; qkss_ready = 2; qkr_ready = 2; qk_ready = 2; qk_turned = 16; qk_copied_a = 8; qk_copied_v = 8
    score_done = 32; max_done = 32; prob_done = 32; pT_done = 32; pT_copied = 32; pv_done = 32; otm_ready = 4; o_turned = 4
    asq_ready = 4; asq_step = 4; ainv_ready = 1; av_scaled = 4; av_turned = 4; vtok_ready = 4
    wsp_masked = 1; wsp_turned = 2; wsp_copied = 2; sv_done = 4
    x_added = 40; f_hi = 32; f_lo = 32; fsq_step = 32
    vector_step = VECTOR_STEPS; scalar_step = SCALAR_STEPS
    bank_read = 27; hidden_read = 17


def delta_schedule():
    for tt in range(TT + 1):
        if tt < TT:
            yield "prep", tt, 0
            yield "gram", tt, 0
        for n in range(6):
            if tt < TT:
                yield "level", tt, n
            if tt > 0 and n < 5:
                yield "rec", tt - 1, n
        if tt < TT:
            yield "solve", tt, 0


def hybrid_trunk(nc, stream, params, x, positions, constants, out):
    with ExitStack() as ctx:
        def sb(name, shape, dt=F32):
            return ctx.enter_context(nc.sbuf_tensor(name, shape, dt))

        def sem(name):
            return ctx.enter_context(nc.semaphore(name))

        hHi, hLo = sb("hHi", [P, KD, SEQ], F32R), sb("hLo", [P, KD, SEQ], F32R)
        wraw = sb("wraw", [P, RAW, UCOLS])
        wHi, wLo = sb("wHi", [P, RING, UCOLS], F32R), sb("wLo", [P, RING, UCOLS], F32R)
        cst, prm = sb("cst", [P, NCST]), sb("prm", [P, NPRM])
        identr, maskr = sb("identr", [P, P], F32R), sb("maskr", [P, 3, P], F32R)
        posi, posf = sb("posi", [P, TT], I32), sb("posf", [P, TT])
        trig = sb("trig", [P, 2, TT, ROPE // 2])
        epsb, epsb64, lnscale = sb("epsb", [P, 1]), sb("epsb64", [P, 1]), sb("lnscale", [P, 1])
        stat, rstd = sb("stat", [P, TT]), sb("rstd", [P, TT])
        token = sb("token", [P, 3, TT, HEADS])
        eglb, egl, expa = sb("eglb", [P, PAIRS, CHUNKS]), sb("egl", [HEADS, CHUNKS]), sb("expa", [HEADS, 1])
        headstat = sb("headstat", [P, 2, TT * HEADS])
        negmax, psums, pinv = sb("negmax", [P, 2]), sb("psums", [P, 2, HEADS]), sb("pinv", [P, HEADS])

        def at(kib, name, shape, dt=F32):
            with ExitStack() as below:
                if kib:
                    below.enter_context(nc.sbuf_tensor(f"below_{name}", [P, kib * 256], F32))
                return below.enter_context(nc.sbuf_tensor(name, shape, dt))

        tile2 = [P, 2, SEQ]
        xs, merged = at(0, "xs", [P, TT, D]), at(16, "merged", [P, KD, SEQ])
        bHi, bLo = at(32, "bHi", [P, 4, SEQ], F32R), at(40, "bLo", [P, 4, SEQ], F32R)
        sg, gy = at(96, "sg", tile2), at(100, "gy", tile2)
        kT, qT = at(0, "kT", [P, PAIRS, SEQ]), at(8, "qT", [P, PAIRS, SEQ])
        vT, qeT = at(16, "vT", [P, PAIRS, SEQ]), at(24, "qeT", [P, PAIRS, SEQ])
        convd, csq = at(40, "convd", tile2), at(44, "csq", tile2)
        rhsk, rhsv, kend = at(32, "rhsk", [P, 512]), at(34, "rhsv", [P, 512]), at(36, "kend", [P, 2, 512])
        unit8 = [P, 2, PAIRS, P]
        LT, X, XT = at(40, "LT", unit8), at(44, "X", unit8), at(48, "XT", unit8)
        Y, CT = at(52, "Y", unit8), at(56, "CT", unit8)
        intra, usol = at(60, "intra", [P, 2, 2, PAIRS, P]), at(68, "usol", [P, 2, 512])
        wsol, vnew = at(72, "wsol", [P, 2, PAIRS, P]), at(76, "vnew", [P, 512])
        state, sdec = at(78, "state", [P, PAIRS, P]), at(80, "sdec", [P, PAIRS, P])
        decay = at(82, "decay", tile2)
        xrow, arow = at(86, "xrow", [P, SEQ]), at(88, "arow", [P, SEQ])
        gcum, lnb = at(90, "gcum", [HEADS, SEQ]), at(92, "lnb", [HEADS, SEQ])
        rowa, rowb = at(94, "rowa", [HEADS, SEQ]), at(96, "rowb", [HEADS, SEQ])
        rowc, rowe = at(98, "rowc", [HEADS, SEQ]), at(100, "rowe", [HEADS, SEQ])
        lnk, lnq = at(102, "lnk", [HEADS, SEQ]), at(104, "lnq", [HEADS, SEQ])
        krT = at(106, "krT", [ROPE, SEQ])
        osq, oinv, szz, bval = at(52, "osq", tile2), at(56, "oinv", tile2), at(60, "szz", tile2), at(64, "bval", tile2)
        latT, lsq, linv = at(48, "latT", [P, 5, SEQ]), at(58, "lsq", tile2), at(62, "linv", tile2)
        latHi, latLo = at(66, "latHi", [P, 5, SEQ], F32R), at(76, "latLo", [P, 5, SEQ], F32R)
        ltmp = at(86, "ltmp", tile2)
        qtm, ktm = at(0, "qtm", [P, TT, HEADS, QK]), at(48, "ktm", [P, TT, HEADS, QK])
        krope, vtm, qksq = at(108, "krope", [P, TT, ROPE]), at(88, "vtm", [P, TT, 512]), at(32, "qksq", [P, TT, HEADS, QK])
        rtmp = at(98, "rtmp", [P, 4, TT, HEADS, ROPE // 2])
        qhT, khT = at(66, "qhT", [P, HEADS, SEQ]), at(0, "khT", [P, HEADS, SEQ])
        prob, probT, otm = at(82, "prob", tile2), at(96, "probT", tile2), at(100, "otm", [P, 2, 512])
        avT, auT, vtok = at(48, "avT", [P, 4, SEQ]), at(56, "auT", [P, 4, SEQ]), at(64, "vtok", [P, TT, 512])
        wspT, asq, ainv, aval = at(72, "wspT", [P, 8, P]), at(76, "asq", tile2), at(80, "ainv", [P, SEQ]), at(82, "aval", tile2)
        xn = at(16, "xn", [P, TT, D])
        fHi = [at(64, "fHi0", [P, 8, SEQ], F32R), at(32, "fHi1", [P, 8, SEQ], F32R)]
        fLo = [at(80, "fLo0", [P, 8, SEQ], F32R), at(48, "fLo1", [P, 8, SEQ], F32R)]
        relu, fsq = at(96, "relu", tile2), at(100, "fsq", tile2)

        ps = ctx.enter_context(nc.psum_tensor("ps", [P, 8, 512], F32))

        def c(name, i=0, n=None, parts=P):
            a, b = CST[name]
            return cst[0:parts, a + i * (n or 0):(a + (i + 1) * n if n else b)]

        def p(name, i=None, parts=P):
            a, b = PRM[name]
            return prm[0:parts, a:b] if i is None else prm[0:parts, a + i:a + i + 1]

        ident = c("ident")

        consts_in, rope_step, consts_done = sem("consts_in"), sem("rope_step"), sem("consts_done")
        raw_loaded = [sem(f"raw{slot}_loaded") for slot in range(RAW)]
        unit_high = sem("unit_high")
        split_begun = sem("split_begun")
        unit_split, unit_done = sem("unit_split"), sem("unit_done")
        x_stored, prm_loaded, x_loaded = sem("x_stored"), sem("prm_loaded"), sem("x_loaded")
        rstd_ready, xn_ready, h_turned, h_hi = sem("rstd_ready"), sem("xn_ready"), sem("h_turned"), sem("h_hi")
        h_lo = sem("h_lo")
        act_tile, csq_ready, csq_summed = sem("act_tile"), sem("csq_ready"), sem("csq_summed")
        soft_abs, soft_ln, soft_done, cum_done = sem("soft_abs"), sem("soft_ln"), sem("soft_done"), sem("cum_done")
        ln_rows, rows_done, egl_done, rows_turned = sem("ln_rows"), sem("rows_done"), sem("egl_done"), sem("rows_turned")
        token_done = sem("token_done")
        qe_bcast, qe_exp, qe_done = sem("qe_bcast"), sem("qe_exp"), sem("qe_done")
        tok_turned, tok_scaled, expo_done, decay_done = sem("tok_turned"), sem("tok_scaled"), sem("expo_done"), sem("decay_done")
        gram_done, gated_done = sem("gram_done"), sem("gated_done")
        xt_first, x_turned, x_first, ct_ready = sem("xt_first"), sem("x_turned"), sem("x_first"), sem("ct_ready")
        y_done, y_copied, z_done, z_added = sem("y_done"), sem("y_copied"), sem("z_done"), sem("z_added")
        solved, sol_copied, ws_done, inter_done = sem("solved"), sem("sol_copied"), sem("ws_done"), sem("inter_done")
        vnew_done, supd_done, state_done, o_done = sem("vnew_done"), sem("supd_done"), sem("state_done"), sem("o_done")
        o_copied = sem("o_copied")
        osq_ready, osq_summed, oinv_ready, on_done = sem("osq_ready"), sem("osq_summed"), sem("oinv_ready"), sem("on_done")
        bval_ready, b_hi, b_lo = sem("bval_ready"), sem("b_hi"), sem("b_lo")
        y_read, m_ready, m_hi, m_lo = sem("y_read"), sem("m_ready"), sem("m_hi"), sem("m_lo")
        lsq_ready, lsq_step, linv_ready, lat_val = sem("lsq_ready"), sem("lsq_step"), sem("linv_ready"), sem("lat_val")
        lat_hi, lat_lo, kr_turned, kr_copied = sem("lat_hi"), sem("lat_lo"), sem("kr_turned"), sem("kr_copied")
        kr_placed = sem("kr_placed")
        up_done, up_copied, qksq_ready, qkss_ready = sem("up_done"), sem("up_copied"), sem("qksq_ready"), sem("qkss_ready")
        qkr_ready, qk_ready, qk_turned, qk_copied_a = sem("qkr_ready"), sem("qk_ready"), sem("qk_turned"), sem("qk_copied_a")
        qk_copied_v = sem("qk_copied_v")
        score_done, max_done, prob_done, pT_done = sem("score_done"), sem("max_done"), sem("prob_done"), sem("pT_done")
        pT_copied, pv_done, otm_ready, o_turned = sem("pT_copied"), sem("pv_done"), sem("otm_ready"), sem("o_turned")
        asq_ready, asq_step, ainv_ready, av_scaled = sem("asq_ready"), sem("asq_step"), sem("ainv_ready"), sem("av_scaled")
        av_turned, vtok_ready, wsp_masked, wsp_turned = sem("av_turned"), sem("vtok_ready"), sem("wsp_masked"), sem("wsp_turned")
        wsp_copied, sv_done = sem("wsp_copied"), sem("sv_done")
        x_added, f_hi, f_lo, fsq_step = sem("x_added"), sem("f_hi"), sem("f_lo"), sem("fsq_step")
        vector_step, scalar_step = sem("vector_step"), sem("scalar_step")
        bank_read, hidden_read = [sem(f"bank_read{bank}") for bank in range(2)], [sem(f"hidden_read{bank}") for bank in range(2)]
        per = PerLayer

        def bank_of(n):
            return ps[:, n % 2]

        block = ctx.enter_context(nc.Block())

        @block.sync
        def _(sp):
            def load_unit(n, slot):
                sp.dma_start(wraw[:, slot], stream[bass.ds(n, 1)].rearrange("a p n -> p (a n)")
                             ).then_inc(raw_loaded[slot], 16)

            for slot in range(RAW):
                load_unit(slot, slot)
            with sp.Fori(1, DEPTH * U // RAW) as turn:
                n = turn * RAW
                for slot in range(RAW):
                    sp.wait_ge(unit_split, n + slot - RAW + 1)
                    load_unit(n + slot, slot)

        @block.gpsimd
        def _(pool):
            def split(slot, loads, done_before):
                raw = slot % RAW
                pool.wait_ge(raw_loaded[raw], 16 * loads)
                pool.sem_inc(split_begun, 1)
                nc.gpsimd.tensor_scalar(wHi[:, slot], wraw[:, raw], 1.0, None, ALU.mult).then_inc(unit_high, 1)
                pool.wait_ge(unit_high, done_before + 1)
                nc.gpsimd.tensor_tensor(wLo[:, slot], wraw[:, raw], wHi[:, slot].bitcast(F32),
                                        ALU.subtract).then_inc(unit_split, 1)

            for slot in range(RING):
                split(slot, slot // RAW + 1, slot)
            with pool.Fori(1, DEPTH * U // RING) as turn:
                n = turn * RING
                for slot in range(RING):
                    pool.wait_ge(unit_done, n + slot - RING + 1)
                    split(slot, turn * (RING // RAW) + (slot // RAW + 1), n + slot)

        @block.tensor
        def _(pe):
            pe.wait_ge(consts_in, 48)
            pe.wait_ge(consts_done, 1)
            with pe.Fori(0, DEPTH) as layer:
                mm = nc.tensor.matmul

                def S(n):
                    return ps[:, 2 + n]

                def passes(o, l, lc, r, rc, start, stop):
                    (lh, ll), (rh, rl) = l, r
                    mm(o, lh[lc], rh[rc], start=start, stop=False)
                    mm(o, lh[lc], rl[rc], start=False, stop=False)
                    return mm(o, ll[lc], rh[rc], start=False, stop=stop)

                def turn_norm(which):
                    pe.wait_ge(xn_ready, layer * per.xn_ready + 4 * which + 4)
                    for k in range(KD):
                        if k >= 4:
                            pe.wait_ge(h_lo, layer * per.h_lo + 8 * which + k - 3)
                        for t in range(TT):
                            last = nc.tensor.transpose(S(k % 4)[:, t * P:(t + 1) * P], xn[:, t, k * P:(k + 1) * P], ident)
                        last.then_inc(h_turned, 1)

                def project(tile):
                    n, u = TILE_NO[tile], UNIT_NO[tile]
                    if n >= 2:
                        pe.wait_ge(bank_read[n % 2], layer * per.bank_read + n // 2)
                    pe.wait_ge(unit_split, layer * per.unit_split + u + 1)
                    slot = u % RING
                    for k in range(KD):
                        if n == 0:
                            pe.wait_ge(h_lo, layer * per.h_lo + k + 1)
                        last = passes(bank_of(n), (wHi, wLo), np.s_[:, slot, k * P:(k + 1) * P], (hHi, hLo), np.s_[:, k], k == 0, k == KD - 1)
                    last.then_inc(unit_done, 1)

                def sum_squares(i):
                    pe.wait_ge(csq_ready, layer * per.csq_ready + i + 1)
                    mm(S(i // 4)[0:HEADS], c("ind", i % 4, 8), csq[:, i % 2], start=i % 4 == 0, stop=i % 4 == 3).then_inc(csq_summed, 1)

                def delta_rows():
                    pe.wait_ge(rows_done, layer * per.rows_done + 1)
                    pe.wait_ge(egl_done, layer * per.egl_done + 1)
                    for j in range(PAIRS):
                        last = mm(S(3)[:, j * 8:j * 8 + 8], c("pair", j, P, 8), egl[:], start=True, stop=True)
                    for kind, row in enumerate((rowa, rowe, lnb)):
                        for t in range(TT):
                            last = nc.tensor.transpose(S(2)[:, (kind * TT + t) * 8:(kind * TT + t) * 8 + 8],
                                                       row[:, t * P:(t + 1) * P], c("ident", parts=8)[:, 0:8])
                    last.then_inc(rows_turned, 1)
                    for j in range(PAIRS):
                        if j >= 2:
                            pe.wait_ge(qe_exp, layer * per.qe_exp + j - 1)
                        mm(S(4 + j % 2), c("pair", j, P, 8), rowc[:], start=True, stop=True).then_inc(qe_bcast, 1)

                def prep(tt):
                    ts = np.s_[tt * P:(tt + 1) * P]
                    if tt == 0:
                        pe.wait_ge(token_done, layer * per.token_done + 1)
                        pe.wait_ge(act_tile, layer * per.act_tile + 12)
                    else:
                        pe.wait_ge(sol_copied, layer * per.sol_copied + 2 * tt)
                    for j in range(PAIRS):
                        last = nc.tensor.transpose(S(0)[:, j * P:(j + 1) * P], kT[:, j, ts], ident)
                    last.then_inc(tok_turned, 1)
                    for j in range(PAIRS):
                        last = nc.tensor.transpose(S(1)[:, j * P:(j + 1) * P], vT[:, j, ts], ident)
                    last.then_inc(tok_turned, 1)

                def gram(tt):
                    ts = np.s_[tt * P:(tt + 1) * P]
                    for n in range(4):
                        kind, par = n // 2, n % 2
                        half = np.s_[64 * par:64 * par + 64]
                        m = 4 * tt + n
                        if n >= 2:
                            pe.wait_ge(decay_done, layer * per.decay_done + m - 1)
                        e = S(2 + par)
                        mm(e, identr[:], maskr[:, kind:kind + 1, :].broadcast_to([P, PAIRS, P]), start=True, stop=False)
                        for j in range(PAIRS):
                            h = 2 * j + par
                            o = e[:, j * P:(j + 1) * P]
                            mm(o, c("sel", h, P, 8), (rowa, rowc)[kind][:, ts], start=False, stop=False)
                            last = mm(o, rowb[:, ts], c("sel", h, P, 8), start=False, stop=j == 3)
                        last.then_inc(expo_done, 1)
                        if n < 2:
                            pe.wait_ge(tok_scaled, layer * per.tok_scaled + 2 * tt + 1 + par)
                        else:
                            pe.wait_ge(gated_done, layer * per.gated_done + m - 1)
                        for j in range(PAIRS):
                            last = mm(S(par)[:, j * P:(j + 1) * P], kT[half, j, ts], (kT, qT)[kind][half, j, ts], start=True, stop=True)
                        last.then_inc(gram_done, 1)

                def level(tt, n):
                    if n == 0:
                        pe.wait_ge(xt_first, layer * per.xt_first + tt + 1)
                        for hf in range(2):
                            for j in range(PAIRS):
                                last = nc.tensor.transpose(S(hf)[:, j * P:(j + 1) * P], XT[:, hf, j], ident)
                            last.then_inc(x_turned, 1)
                        return
                    m = 10 * tt + 2 * (n - 1)
                    pe.wait_ge(ct_ready, layer * per.ct_ready + 5 * tt + n)
                    for hf in range(2):
                        if n == 1:
                            pe.wait_ge(x_first, layer * per.x_first + 2 * tt + hf + 1)
                        else:
                            pe.wait_ge(z_added, layer * per.z_added + m + hf - 1)
                        for j in range(PAIRS):
                            last = mm(S(hf)[:, j * P:(j + 1) * P], CT[:, hf, j], X[:, hf, j], start=True, stop=True)
                        last.then_inc(y_done, 1)
                    for hf in range(2):
                        pe.wait_ge(y_copied, layer * per.y_copied + m + hf + 1)
                        if hf:
                            pe.wait_ge(z_added, layer * per.z_added + m + 1)
                        for j in range(PAIRS):
                            last = mm(S(2)[:, j * P:(j + 1) * P], Y[:, hf, j], XT[:, hf, j], start=True, stop=True)
                        if n < 5:
                            for j in range(PAIRS):
                                last = mm(S(3)[:, j * P:(j + 1) * P], XT[:, hf, j], Y[:, hf, j], start=True, stop=True)
                        last.then_inc(z_done, 1)

                def solve(tt):
                    pe.wait_ge(z_added, layer * per.z_added + 10 * tt + 10)
                    for h in range(HEADS):
                        last = mm(S(0)[:, h * 64:h * 64 + 64], XT[:, h % 2, h // 2], rhsv[:, h * 64:h * 64 + 64], start=True, stop=True)
                    last.then_inc(solved, 1)
                    for h in range(HEADS):
                        last = mm(S(1)[64 * (h % 2):64 * (h % 2) + 64, h // 2 * P:(h // 2 + 1) * P],
                                  rhsk[:, h * 64:h * 64 + 64], XT[:, h % 2, h // 2], start=True, stop=True)
                    last.then_inc(solved, 1)

                def recur(tt, part):
                    half = part // 2
                    hs = np.s_[64 * half:64 * half + 64]
                    m = 2 * tt + half
                    if part in (0, 2):
                        if part == 0:
                            pe.wait_ge(sol_copied, layer * per.sol_copied + 2 * tt + 2)
                            if tt:
                                pe.wait_ge(o_copied, layer * per.o_copied + tt)
                        if m:
                            pe.wait_ge(state_done, layer * per.state_done + m)
                        for j in range(PAIRS):
                            last = mm(S(4)[hs, j * P:(j + 1) * P], wsol[:, tt % 2, j, hs], state[:, j], start=True, stop=True)
                        last.then_inc(ws_done, 1)
                        for j in range(PAIRS):
                            t0 = j * P + 64 * half
                            last = mm(bank_of(1)[:, t0:t0 + 64], state[:, j], qeT[:, j, tt * P + 64 * half:tt * P + 64 * half + 64],
                                      start=part == 0 and j == 0, stop=False, skip_group_check=True)
                        last.then_inc(inter_done, 1)
                    elif part in (1, 3):
                        pe.wait_ge(vnew_done, layer * per.vnew_done + m + 1)
                        for j in range(PAIRS):
                            last = mm(S(5)[:, j * P:(j + 1) * P], kend[hs, tt % 2, j * P:(j + 1) * P], vnew[hs, j * P:(j + 1) * P],
                                      start=True, stop=True)
                        last.then_inc(supd_done, 1)
                    else:
                        for h in range(HEADS):
                            last = mm(bank_of(1)[64 * (h % 2):64 * (h % 2) + 64, h // 2 * P:(h // 2 + 1) * P],
                                      vnew[:, h * 64:h * 64 + 64], intra[:, tt % 2, h % 2, h // 2], start=False, stop=h == 7,
                                      skip_group_check=True)
                        last.then_inc(o_done, 1)

                def branch_out(br, first):
                    pe.wait_ge(b_lo, layer * per.b_lo + 4 * first + 4)
                    for d2 in range(4):
                        u = UNIT_NO[(f"y{br}", d2)]
                        slot = u % RING
                        pe.wait_ge(unit_split, layer * per.unit_split + u + 1)
                        for i in range(2):
                            n = 8 * first + 2 * d2 + i
                            if n >= 2:
                                pe.wait_ge(y_read, layer * per.y_read + n - 1)
                            for k in range(4):
                                last = passes(S(4 + i), (wHi, wLo), np.s_[:, slot, k * 256 + i * P:k * 256 + (i + 1) * P],
                                              (bHi, bLo), np.s_[:, k], k == 0, k == 3)
                        last.then_inc(unit_done, 1)
                        project((f"gate{br}", 2 * d2))
                        project((f"gate{br}", 2 * d2 + 1))

                turn_norm(0)

                project(("misc", 0))
                for i in range(12):
                    project((("k", "q", "v")[i // 4], i % 4))
                    if 2 <= i < 10:
                        sum_squares(i - 2)
                delta_rows()
                for stage, tt, n in delta_schedule():
                    if stage == "prep":
                        prep(tt)
                    elif stage == "gram":
                        gram(tt)
                    elif stage == "level":
                        level(tt, n)
                    elif stage == "solve":
                        solve(tt)
                    else:
                        recur(tt, n)
                for j in range(4):
                    pe.wait_ge(osq_ready, layer * per.osq_ready + j + 1)
                    if j >= 2:
                        pe.wait_ge(oinv_ready, layer * per.oinv_ready + j - 1)
                    mm(S(j % 2), c("block"), osq[:, j % 2], start=True, stop=True).then_inc(osq_summed, 1)
                for j in range(4):
                    project(("z", j))
                branch_out(2, 0)

                for j in range(5):
                    project(("lat", j))
                for j in range(5):
                    pe.wait_ge(lsq_ready, layer * per.lsq_ready + j + 1)
                    last = mm(S(0 if j < 3 else 1), c("ones"), lsq[:, j % 2], start=j in (0, 3), stop=j in (2, 4))
                    last.then_inc(lsq_step, 1)
                for t in range(TT):
                    last = nc.tensor.transpose(S(2)[:, t * ROPE:(t + 1) * ROPE], krT[:, t * P:(t + 1) * P], c("ident", parts=ROPE)[:, 0:ROPE])
                last.then_inc(kr_turned, 1)
                for n in range(6):
                    u = UNIT_NO[("qup", n)] if n < 4 else UNIT_NO[("kvup", n - 4)]
                    k0, nk, w = (0, 3, 192) if n < 4 else (3, 2, 512)
                    slot = u % RING
                    pe.wait_ge(unit_split, layer * per.unit_split + u + 1)
                    pe.wait_ge(lat_lo, layer * per.lat_lo + k0 + nk)
                    for t in range(TT):
                        g = n * 2 + t // 2 if n < 4 else 8 + (n - 4) * 4 + t
                        if (n >= 4 or t % 2 == 0) and g >= 4:
                            pe.wait_ge(up_copied, layer * per.up_copied + g - 3)
                        if (n, t) in ((0, 2), (1, 0)):
                            pe.wait_ge(kr_copied, layer * per.kr_copied + 1)
                            pe.wait_ge(linv_ready, layer * per.linv_ready + 2)
                        o = S(g % 4)[:, (t % 2) * 192:(t % 2) * 192 + 192] if n < 4 else S(g % 4)
                        for k in range(nk):
                            last = passes(o, (latHi, latLo), np.s_[:, k0 + k, t * P:(t + 1) * P],
                                          (wHi, wLo), np.s_[:, slot, k * w:(k + 1) * w], k == 0, k == nk - 1)
                        if t == TT - 1:
                            last.then_inc(unit_done, 1)
                        elif n >= 4 or t % 2:
                            last.then_inc(up_done, 1)
                for n in range(16):
                    if n % 8 == 0:
                        pe.wait_ge(qk_ready, layer * per.qk_ready + n // 8 + 1)
                    src = (qtm, ktm)[n // 8]
                    if n >= 4:
                        pe.wait_ge(qk_copied_v if n % 2 else qk_copied_a, layer * per.qk_copied_v + n // 2 - 1)
                    for t in range(TT):
                        last = nc.tensor.transpose(S(n % 4)[0:QK, t * P:(t + 1) * P], src[:, t, n % 8], ident)
                    last.then_inc(qk_turned, 1)
                pe.wait_ge(qk_copied_a, layer * per.qk_copied_a + 8)
                pe.wait_ge(qk_copied_v, layer * per.qk_copied_v + 8)

                def scores(n):
                    i, h = n // 8, n % 8
                    w = (i + 1) * P
                    if n >= 2:
                        pe.wait_ge(prob_done, layer * per.prob_done + n - 1)
                    bank = S(n % 2)
                    mm(bank[:, 0:w], qhT[0:QK, h, i * P:w], khT[0:QK, h, 0:w], start=True, stop=False)
                    mm(bank[:, i * P:w], identr[:], maskr[:, 2], start=False, stop=True).then_inc(score_done, 1)

                def turn_probs(n):
                    pe.wait_ge(prob_done, layer * per.prob_done + n + 1)
                    if n >= 2:
                        pe.wait_ge(pT_copied, layer * per.pT_copied + n - 1)
                    for kb in range(n // 8 + 1):
                        last = nc.tensor.transpose(S(2 + n % 2)[:, kb * P:(kb + 1) * P], prob[:, n % 2, kb * P:(kb + 1) * P], ident)
                    last.then_inc(pT_done, 1)

                def weigh(n):
                    i, h = n // 8, n % 8
                    pe.wait_ge(pT_copied, layer * per.pT_copied + n + 1)
                    if h == 0 and i >= 2:
                        pe.wait_ge(otm_ready, layer * per.otm_ready + i - 1)
                    for kb in range(i + 1):
                        last = mm(S(4 + i % 2)[:, h * 64:h * 64 + 64], probT[:, n % 2, kb * P:(kb + 1) * P],
                                  vtm[:, kb, h * 64:h * 64 + 64], start=kb == 0, stop=kb == i)
                    last.then_inc(pv_done, 1)

                def turn_outputs(i):
                    pe.wait_ge(otm_ready, layer * per.otm_ready + i + 1)
                    if i >= 2:
                        pe.wait_ge(b_lo, layer * per.b_lo + 4 + i - 1)
                    for j in range(4):
                        last = nc.tensor.transpose(bank_of(i)[:, j * P:(j + 1) * P], otm[:, i % 2, j * P:(j + 1) * P], ident)
                    last.then_inc(o_turned, 1)

                for n in range(32 + 2):
                    if n < 32:
                        scores(n)
                    if 1 <= n <= 32:
                        turn_probs(n - 1)
                    if n >= 2:
                        weigh(n - 2)
                    if n % 8 == 4 and n > 8:
                        turn_outputs(n // 8 - 1)
                turn_outputs(3)
                branch_out(1, 1)

                for j in range(4):
                    project(("av", j))
                for j in range(4):
                    pe.wait_ge(asq_ready, layer * per.asq_ready + j + 1)
                    mm(S(0), c("ones"), asq[:, j % 2], start=j == 0, stop=j == 3).then_inc(asq_step, 1)
                pe.wait_ge(wsp_masked, layer * per.wsp_masked + 1)
                for g in range(8):
                    last = nc.tensor.transpose(S(1 + g // 4)[:, g % 4 * P:(g % 4 + 1) * P], p("wsp")[:, g * P:(g + 1) * P], ident)
                    if g % 4 == 3:
                        last.then_inc(wsp_turned, 1)
                for j in range(4):
                    project(("au", j))
                pe.wait_ge(av_scaled, layer * per.av_scaled + 4)
                pe.wait_ge(wsp_copied, layer * per.wsp_copied + 2)
                pe.wait_ge(ainv_ready, layer * per.ainv_ready + 1)
                for t in range(TT):
                    if t >= 2:
                        pe.wait_ge(vtok_ready, layer * per.vtok_ready + t - 1)
                    for j in range(4):
                        last = nc.tensor.transpose(S(t % 2)[:, j * P:(j + 1) * P], avT[:, j, t * P:(t + 1) * P], ident)
                    last.then_inc(av_turned, 1)
                pe.wait_ge(vtok_ready, layer * per.vtok_ready + 4)
                for j in range(4):
                    if j >= 2:
                        pe.wait_ge(bval_ready, layer * per.bval_ready + 4 + j - 1)
                    o = S(2 + j % 2)
                    mm(o, c("pair", j, P, 8), p("bsp", parts=8).unsqueeze(1).broadcast_to([8, TT, P]), start=True, stop=False,
                       skip_group_check=True)
                    for t in range(TT):
                        for par in range(2):
                            g = 2 * j + par
                            last = mm(o[64 * par:64 * par + 64, t * P:(t + 1) * P], vtok[:, t, g * 64:g * 64 + 64], wspT[:, g],
                                      start=False, stop=t == 3, skip_group_check=True)
                    last.then_inc(sv_done, 1)
                branch_out(0, 2)

                for half in range(2):
                    for kk in range(4):
                        u = UNIT_NO[("out", 4 * half + kk)]
                        slot = u % RING
                        pe.wait_ge(unit_split, layer * per.unit_split + u + 1)
                        pe.wait_ge(m_lo, layer * per.m_lo + 2 * kk + 2)
                        if half and kk == 0:
                            pe.wait_ge(y_read, layer * per.y_read + 24)
                        for t in range(TT):
                            o = ps[:, (2 + 4 * half + t) % 8]
                            for i in range(2):
                                k = 2 * kk + i
                                last = passes(o, (fHi[0], fLo[0]), np.s_[:, k, t * P:(t + 1) * P],
                                              (wHi, wLo), np.s_[:, slot, i * 512:(i + 1) * 512], k == 0, k == 7)
                        last.then_inc(unit_done, 1)
                turn_norm(1)

                with pe.Fori(0, 2) as q2:
                    for b in range(2):
                        q = q2 * 2 + b
                        for f in range(8):
                            slot = f % RING
                            pe.wait_ge(hidden_read[f % 2], layer * per.hidden_read + q * 4 + f // 2 + 1)
                            pe.wait_ge(unit_split, layer * per.unit_split + q * 16 + (FF0 + f + 1))
                            for k in range(KD):
                                last = passes(bank_of(f), (wHi, wLo), np.s_[:, slot, k * P:(k + 1) * P], (hHi, hLo), np.s_[:, k], k == 0, k == KD - 1)
                            last.then_inc(unit_done, 1)
                        for half in range(2):
                            for kk in range(4):
                                slot = kk % RING
                                pe.wait_ge(unit_split, layer * per.unit_split + q * 16 + (FF0 + 8 + 4 * half + kk + 1))
                                if half == 0:
                                    pe.wait_ge(f_lo, layer * per.f_lo + q * 8 + (2 * kk + 2))
                                    if kk == 0:
                                        pe.wait_ge(x_added, layer * per.x_added + q * 8 + 8)
                                for t in range(TT):
                                    if half and kk == 0 and t >= 2:
                                        pe.wait_ge(x_added, layer * per.x_added + q * 8 + (8 + t - 1))
                                    o = S((4 * half + t) % 6)
                                    for i in range(2):
                                        k = 2 * kk + i
                                        last = passes(o, (fHi[b], fLo[b]), np.s_[:, k, t * P:(t + 1) * P],
                                                      (wHi, wLo), np.s_[:, slot, i * 512:(i + 1) * 512], k == 0, k == 7)
                                last.then_inc(unit_done, 1)

        @block.scalar
        def _(act):
            act.dma_start(cst[:], constants).then_inc(consts_in, 16)
            act.dma_start(posi[:], positions).then_inc(consts_in, 16)
            act.dma_start(xs[:], x.rearrange("(t p) d -> p t d", p=P)).then_inc(consts_in, 16)
            act.dma_start(prm[:], params[0]).then_inc(prm_loaded, 16)
            act.wait_ge(consts_in, 48)
            act.dma_start(out.rearrange("(t p) d -> p t d", p=P), xs[:]).then_inc(x_stored, 16)
            nc.scalar.copy(identr[:], ident)
            nc.scalar.copy(maskr[:, 0], c("strict"))
            nc.scalar.copy(maskr[:, 1], c("incl"))
            nc.scalar.copy(maskr[:, 2], c("causal"))
            act.wait_ge(rope_step, ROPE_STEPS)
            nc.scalar.activation(trig[:], trig[:], ACT.Sin).then_inc(consts_done, 1)
            with act.Fori(0, DEPTH) as layer:
                steps = Steps()
                f = nc.scalar.activation

                def S(n):
                    return ps[:, 2 + n]

                def norm_stats(which):
                    for t in range(TT):
                        if which:
                            act.wait_ge(x_added, layer * per.x_added + 4 + t + 1)
                        last = f(xn[:, t], xs[:, t], ACT.Square, accum_out=stat[:, t:t + 1])
                    last.then_inc(scalar_step, 1)
                    act.wait_ge(scalar_step, layer * per.scalar_step + steps.next())
                    f(stat[:], stat[:], ACT.Ln, bias=epsb[:], scale=1.0 / D).then_inc(scalar_step, 1)
                    act.wait_ge(scalar_step, layer * per.scalar_step + steps.next())
                    f(rstd[:], stat[:], ACT.Exp, scale=-0.5).then_inc(rstd_ready, 1)

                def norm_high(which):
                    for k in range(KD):
                        act.wait_ge(h_turned, layer * per.h_turned + 8 * which + k + 1)
                        if k == 0 and which == 0:
                            act.wait_ge(prm_loaded, layer * per.prm_loaded + 16)
                        f(hHi[:, k], S(k % 4), ACT.Copy, scale=p("g2" if which else "g1", k)).then_inc(h_hi, 1)

                def inverse_root(o, i, scale):
                    f(o, i, ACT.Ln, bias=epsb[0:o.shape[0]], scale=scale).then_inc(scalar_step, 1)
                    act.wait_ge(scalar_step, layer * per.scalar_step + steps.next())
                    return f(o, o, ACT.Exp, scale=-0.5)

                def branch_gates(br, first):
                    for d in range(KD):
                        tile = (f"gate{br}", d)
                        act.wait_ge(unit_done, layer * per.unit_done + UNIT_NO[tile] + 1)
                        n = 8 * first + d
                        if n >= 2:
                            act.wait_ge(y_read, layer * per.y_read + n - 1)
                        f(sg[:, d % 2], bank_of(TILE_NO[tile]), ACT.Sigmoid).then_inc(bank_read[TILE_NO[tile] % 2], 1)
                        if first == 2 and d >= 1:
                            act.wait_ge(m_ready, layer * per.m_ready + d)
                            nc.scalar.copy(fHi[0][:, d - 1], merged[:, d - 1]).then_inc(m_hi, 1)
                    if first == 2:
                        act.wait_ge(m_ready, layer * per.m_ready + 8)
                        nc.scalar.copy(fHi[0][:, 7], merged[:, 7]).then_inc(m_hi, 1)

                norm_stats(0)
                norm_high(0)

                act.wait_ge(x_stored, layer * per.x_stored + 16)
                for i in range(12):
                    name, j = ("k", "q", "v")[i // 4], i % 4
                    n = TILE_NO[(name, j)]
                    act.wait_ge(bank_read[n % 2], layer * per.bank_read + n // 2 + 1)
                    dst = (kT, qT, vT)[i // 4][:, j]
                    f(dst, convd[:, i % 2], ACT.Silu).then_inc(act_tile, 1)
                    if i < 8:
                        act.wait_ge(act_tile, layer * per.act_tile + i + 1)
                        if i >= 2:
                            act.wait_ge(csq_summed, layer * per.csq_summed + i - 1)
                        f(csq[:, i % 2], dst, ACT.Square).then_inc(csq_ready, 1)
                act.wait_ge(soft_abs, layer * per.soft_abs + 1)
                f(arow[0:40], arow[0:40], ACT.Exp, scale=-1.0).then_inc(scalar_step, 1)
                act.wait_ge(scalar_step, layer * per.scalar_step + steps.next())
                f(expa[:], p("alog", parts=HEADS), ACT.Exp).then_inc(scalar_step, 1)
                act.wait_ge(scalar_step, layer * per.scalar_step + steps.next())
                f(arow[0:40], arow[0:40], ACT.Ln, bias=1.0).then_inc(soft_ln, 1)
                act.wait_ge(csq_summed, layer * per.csq_summed + 8)
                f(lnk[:], S(0)[0:HEADS], ACT.Ln, bias=epsb[0:HEADS])
                f(lnq[:], S(1)[0:HEADS], ACT.Ln, bias=epsb64[0:HEADS], scale=float(CDIM))
                act.wait_ge(soft_done, layer * per.soft_done + 1)
                f(lnb[:], xrow[32:40], ACT.Copy, scale=-1.0).then_inc(ln_rows, 1)
                act.wait_ge(cum_done, layer * per.cum_done + 1)
                f(egl[:], gcum[:].rearrange("h (n t) -> h n t", t=CHUNK)[:, :, CHUNK - 1], ACT.Exp).then_inc(egl_done, 1)
                act.wait_ge(rows_turned, layer * per.rows_turned + 1)
                nc.scalar.copy(eglb[:], S(3)[:, 0:PAIRS * CHUNKS].rearrange("p (j n) -> p j n", j=PAIRS))
                f(token[:], S(2)[:, 0:3 * TT * HEADS].rearrange("p (a t h) -> p a t h", a=3, t=TT), ACT.Exp).then_inc(token_done, 1)
                for j in range(PAIRS):
                    act.wait_ge(qe_bcast, layer * per.qe_bcast + j + 1)
                    if j >= 2:
                        act.wait_ge(qe_done, layer * per.qe_done + j - 1)
                    f(decay[:, j % 2], S(4 + j % 2), ACT.Exp).then_inc(qe_exp, 1)

                for stage, tt, n in delta_schedule():
                    if stage == "gram":
                        for i in range(4):
                            m = 4 * tt + i
                            act.wait_ge(expo_done, layer * per.expo_done + m + 1)
                            if m < 2:
                                act.wait_ge(qe_done, layer * per.qe_done + 4)
                            else:
                                act.wait_ge(gated_done, layer * per.gated_done + m - 1)
                            f(decay[:, i % 2], S(2 + i % 2), ACT.Exp).then_inc(decay_done, 1)
                    elif stage == "level" and n == 0:
                        for hf in range(2):
                            act.wait_ge(x_turned, layer * per.x_turned + 2 * tt + hf + 1)
                            nc.scalar.copy(X[:, hf].rearrange("p j n -> p (j n)"), S(hf)).then_inc(x_first, 1)
                    elif stage == "level":
                        for hf in range(2):
                            m = 10 * tt + 2 * (n - 1) + hf
                            act.wait_ge(y_done, layer * per.y_done + m + 1)
                            nc.scalar.copy(Y[:, hf].rearrange("p j n -> p (j n)"), S(hf)).then_inc(y_copied, 1)
                    elif stage == "solve":
                        act.wait_ge(solved, layer * per.solved + 2 * tt + 1)
                        nc.scalar.copy(usol[:, tt % 2], S(0)).then_inc(sol_copied, 1)
                        act.wait_ge(solved, layer * per.solved + 2 * tt + 2)
                        nc.scalar.copy(wsol[:, tt % 2].rearrange("p j n -> p (j n)"), S(1)).then_inc(sol_copied, 1)
                    elif stage == "rec" and n == 4:
                        act.wait_ge(o_done, layer * per.o_done + tt + 1)
                        nc.scalar.copy(vT[:, :, tt * P:(tt + 1) * P], bank_of(1).rearrange("p (j n) -> p j n", j=PAIRS)).then_inc(o_copied, 1)
                act.wait_ge(o_copied, layer * per.o_copied + 4)
                for j in range(4):
                    if j >= 2:
                        act.wait_ge(osq_summed, layer * per.osq_summed + j - 1)
                    f(osq[:, j % 2], vT[:, j], ACT.Square).then_inc(osq_ready, 1)
                for j in range(4):
                    act.wait_ge(osq_summed, layer * per.osq_summed + j + 1)
                    if j >= 2:
                        act.wait_ge(on_done, layer * per.on_done + j - 1)
                    inverse_root(oinv[:, j % 2], S(j % 2), 1.0 / VDIM).then_inc(oinv_ready, 1)
                for j in range(4):
                    act.wait_ge(unit_done, layer * per.unit_done + UNIT_NO[("z", j)] + 1)
                    if j >= 2:
                        act.wait_ge(bval_ready, layer * per.bval_ready + j - 1)
                    f(szz[:, j % 2], bank_of(TILE_NO[("z", j)]), ACT.Silu).then_inc(bank_read[TILE_NO[("z", j)] % 2], 1)
                    if j >= 1:
                        act.wait_ge(bval_ready, layer * per.bval_ready + j)
                        nc.scalar.copy(bHi[:, j - 1], bval[:, (j - 1) % 2]).then_inc(b_hi, 1)
                act.wait_ge(bval_ready, layer * per.bval_ready + 4)
                nc.scalar.copy(bHi[:, 3], bval[:, 1]).then_inc(b_hi, 1)
                branch_gates(2, 0)

                for j in range(5):
                    act.wait_ge(unit_done, layer * per.unit_done + UNIT_NO[("lat", j)] + 1)
                    n = TILE_NO[("lat", j)]
                    nc.scalar.copy(latT[:, j], bank_of(n)).then_inc(bank_read[TILE_NO[("lat", j)] % 2], 1)
                    act.wait_ge(bank_read[n % 2], layer * per.bank_read + n // 2 + 1)
                    if j >= 2:
                        act.wait_ge(lsq_step, layer * per.lsq_step + j - 1)
                    f(lsq[:, j % 2], latT[:, j], ACT.Square).then_inc(lsq_ready, 1)
                act.wait_ge(lsq_step, layer * per.lsq_step + 3)
                inverse_root(linv[:, 0], S(0), 1.0 / Q_LORA).then_inc(linv_ready, 1)
                act.wait_ge(lsq_step, layer * per.lsq_step + 5)
                inverse_root(linv[:, 1], S(1), 1.0 / KV_LORA).then_inc(linv_ready, 1)
                for j in range(5):
                    act.wait_ge(lat_val, layer * per.lat_val + j + 1)
                    nc.scalar.copy(latHi[:, j], ltmp[:, j % 2]).then_inc(lat_hi, 1)
                act.wait_ge(kr_turned, layer * per.kr_turned + 1)
                nc.scalar.copy(krope[:], S(2)[:, 0:TT * ROPE].rearrange("p (t r) -> p t r", t=TT)).then_inc(kr_copied, 1)
                seen = 0
                for n in range(6):
                    for t in range(TT):
                        if n < 4 and t % 2 == 0:
                            continue
                        if t == TT - 1:
                            act.wait_ge(unit_done, layer * per.unit_done + UNIT_NO[("qup", n) if n < 4 else ("kvup", n - 4)] + 1)
                        else:
                            seen += 1
                            act.wait_ge(up_done, layer * per.up_done + seen)
                        if n < 4:
                            g = n * 2 + t // 2
                            src = S(g % 4)[:, 0:384].rearrange("p (t h c) -> p t h c", t=2, h=2)
                            ins = nc.scalar.copy(qtm[:, t - 1:t + 1, 2 * n:2 * n + 2], src)
                        else:
                            g = 8 + (n - 4) * 4 + t
                            src = S(g % 4).rearrange("p (h c) -> p h c", h=4)
                            h0 = 4 * (n - 4)
                            nc.scalar.copy(ktm[:, t, h0:h0 + 4, 0:NOPE], src[:, :, 0:NOPE])
                            ins = nc.scalar.copy(vtm[:, t, h0 * 64:h0 * 64 + 256].rearrange("p (h c) -> p h c", h=4), src[:, :, NOPE:])
                        ins.then_inc(up_copied, 1)
                for n in range(2):
                    if n == 0:
                        act.wait_ge(up_copied, layer * per.up_copied + 16)
                    else:
                        act.wait_ge(kr_placed, layer * per.kr_placed + 1)
                        act.wait_ge(qkss_ready, layer * per.qkss_ready + 1)
                    f(qksq[:], (qtm, ktm)[n][:], ACT.Square).then_inc(qksq_ready, 1)
                for n in range(2):
                    act.wait_ge(qkss_ready, layer * per.qkss_ready + n + 1)
                    f(headstat[:, n], headstat[:, n], ACT.Ln, bias=epsb[:], scale=1.0 / QK).then_inc(scalar_step, 1)
                    act.wait_ge(scalar_step, layer * per.scalar_step + steps.next())
                    f(headstat[:, n], headstat[:, n], ACT.Exp, scale=-0.5, bias=lnscale[:] if n == 0 else 0.0).then_inc(qkr_ready, 1)
                for n in range(0, 16, 2):
                    act.wait_ge(qk_turned, layer * per.qk_turned + n + 1)
                    nc.scalar.copy((qhT, khT)[n // 8][0:QK, n % 8], S(n % 4)[0:QK]).then_inc(qk_copied_a, 1)
                def outputs_high(i):
                    act.wait_ge(o_turned, layer * per.o_turned + i + 1)
                    nc.scalar.copy(bHi[:, :, i * P:(i + 1) * P], bank_of(i).rearrange("p (j n) -> p j n", j=4)).then_inc(b_hi, 1)

                for n in range(32):
                    w = (n // 8 + 1) * P
                    act.wait_ge(max_done, layer * per.max_done + n + 1)
                    if n >= 2:
                        act.wait_ge(pT_done, layer * per.pT_done + n - 1)
                    f(prob[:, n % 2, 0:w], S(n % 2)[:, 0:w], ACT.Exp, bias=negmax[:, n % 2:n % 2 + 1],
                                        accum_out=psums[:, n // 8 % 2, n % 8:n % 8 + 1]).then_inc(prob_done, 1)
                    if n % 8 == 5 and n > 8:
                        outputs_high(n // 8 - 1)
                outputs_high(3)
                act.wait_ge(unit_done, layer * per.unit_done + UNIT_NO[("y1", 0)] + 1)
                act.wait_ge(x_stored, layer * per.x_stored + 16)
                act.dma_start(xs[:], out.rearrange("(t p) d -> p t d", p=P)).then_inc(x_loaded, 16)
                branch_gates(1, 1)

                for j in range(4):
                    act.wait_ge(unit_done, layer * per.unit_done + UNIT_NO[("av", j)] + 1)
                    n = TILE_NO[("av", j)]
                    f(avT[:, j], bank_of(n), ACT.Gelu).then_inc(bank_read[TILE_NO[("av", j)] % 2], 1)
                    act.wait_ge(bank_read[n % 2], layer * per.bank_read + n // 2 + 1)
                    if j >= 2:
                        act.wait_ge(asq_step, layer * per.asq_step + j - 1)
                    f(asq[:, j % 2], avT[:, j], ACT.Square).then_inc(asq_ready, 1)
                for j in range(4):
                    act.wait_ge(unit_done, layer * per.unit_done + UNIT_NO[("au", j)] + 1)
                    f(auT[:, j], bank_of(TILE_NO[("au", j)]), ACT.Gelu).then_inc(bank_read[TILE_NO[("au", j)] % 2], 1)
                act.wait_ge(asq_step, layer * per.asq_step + 4)
                inverse_root(ainv[:], S(0), 1.0 / A_WIDTH).then_inc(ainv_ready, 1)
                for g in range(2):
                    act.wait_ge(wsp_turned, layer * per.wsp_turned + g + 1)
                    nc.scalar.copy(wspT[:, 4 * g:4 * g + 4].rearrange("p g n -> p (g n)"), S(1 + g)).then_inc(wsp_copied, 1)
                for j in range(4):
                    act.wait_ge(bval_ready, layer * per.bval_ready + 4 + j + 1)
                    nc.scalar.copy(bHi[:, j], aval[:, j % 2]).then_inc(b_hi, 1)
                branch_gates(0, 2)

                norm_stats(1)
                norm_high(1)
                act.wait_ge(h_lo, layer * per.h_lo + 16)
                act.sem_inc(hidden_read[0], 1)
                act.sem_inc(hidden_read[1], 1)
                with act.Fori(0, 2) as q2:
                    for b in range(2):
                        q = q2 * 2 + b
                        for n in range(8):
                            act.wait_ge(unit_done, layer * per.unit_done + q * 16 + (FF0 + n + 1))
                            if n >= 2:
                                act.wait_ge(f_lo, layer * per.f_lo + q * 8 + (n - 1))
                            f(relu[:, n % 2], bank_of(n), ACT.Relu).then_inc(hidden_read[n % 2], 1)
                            act.wait_ge(hidden_read[n % 2], layer * per.hidden_read + q * 4 + (n // 2 + 2))
                            if n == 0:
                                act.wait_ge(unit_done, layer * per.unit_done + q * 16 + (FF0 - 16))
                            f(fHi[b][:, n], relu[:, n % 2], ACT.Square).then_inc(f_hi, 1)
                act.wait_ge(x_added, layer * per.x_added + 40)
                act.dma_start(out.rearrange("(t p) d -> p t d", p=P), xs[:]).then_inc(x_stored, 16)
                act.dma_start(prm[:], params[bass.ds(layer + 1, 1)].rearrange("a p n -> p (a n)")).then_inc(prm_loaded, 16)
                assert steps.n == SCALAR_STEPS or not SCALAR_STEPS, ("SCALAR_STEPS", steps.n)
            act.wait_ge(x_stored, 16 * (DEPTH + 1))
            act.wait_ge(prm_loaded, 16 * (DEPTH + 1))

        @block.vector
        def _(dve):
            turns = Steps()
            nc.vector.memset(epsb[:], EPS)
            nc.vector.memset(epsb64[:], CDIM * EPS)
            nc.vector.memset(lnscale[:], float(np.log(QK ** -0.5)))
            dve.wait_ge(consts_in, 48)
            nc.vector.tensor_copy(posf[:], posi[:]).then_inc(rope_step, 1)
            dve.wait_ge(rope_step, turns.next())
            ang = [gy[:, n, 0:TT * 16].rearrange("p (t r) -> p t r", t=TT) for n in range(2)]
            cyc = sg[:, 0, 0:TT * 16].rearrange("p (t r) -> p t r", t=TT)
            for n in range(2):
                nc.vector.tensor_tensor(ang[n], posf[:].unsqueeze(2).broadcast_to([P, TT, 16]),
                                                   c("freq").unsqueeze(1).broadcast_to([P, TT, 16]), ALU.mult).then_inc(rope_step, 1)
                dve.wait_ge(rope_step, turns.next())
                nc.vector.tensor_scalar(cyc, ang[n], float(1 / (2 * np.pi)), 0.25 * n, ALU.mult, ALU.add).then_inc(rope_step, 1)
                dve.wait_ge(rope_step, turns.next())
                nc.vector.tensor_scalar(cyc, cyc, ROUND, -ROUND, ALU.add, ALU.add).then_inc(rope_step, 1)
                dve.wait_ge(rope_step, turns.next())
                for part in TWO_PI:
                    nc.vector.scalar_tensor_tensor(ang[n], cyc, -part, ang[n], ALU.mult, ALU.add).then_inc(rope_step, 1)
                    dve.wait_ge(rope_step, turns.next())
                if n:
                    nc.vector.tensor_scalar(ang[n], ang[n], float(np.pi / 2), None, ALU.add).then_inc(rope_step, 1)
                    dve.wait_ge(rope_step, turns.next())
                nc.vector.tensor_scalar(trig[:, n], ang[n], 3.1415925, -3.1415925, ALU.min, ALU.max).then_inc(rope_step, 1)
                dve.wait_ge(rope_step, turns.next())
            assert turns.n == ROPE_STEPS, turns.n
            with dve.Fori(0, DEPTH) as layer:
                steps = Steps()
                tt_, ts_, stt = nc.vector.tensor_tensor, nc.vector.tensor_scalar, nc.vector.scalar_tensor_tensor

                def S(n):
                    return ps[:, 2 + n]

                def scale_x(which):
                    dve.wait_ge(rstd_ready, layer * per.rstd_ready + which + 1)
                    for t in range(TT):
                        ts_(xn[:, t], xs[:, t], rstd[:, t:t + 1], None, ALU.mult).then_inc(xn_ready, 1)

                def norm_low(which):
                    for k in range(KD):
                        dve.wait_ge(h_hi, layer * per.h_hi + 8 * which + k + 1)
                        stt(hLo[:, k], S(k % 4), p("g2" if which else "g1", k), hHi[:, k].bitcast(F32), ALU.mult, ALU.subtract).then_inc(h_lo, 1)

                def branch_merge(br, first):
                    for d in range(KD):
                        n = TILE_NO[(f"gate{br}", d)]
                        dve.wait_ge(bank_read[n % 2], layer * per.bank_read + n // 2 + 1)
                        dst = merged[:, d] if first == 0 else gy[:, d % 2]
                        ins = tt_(dst, sg[:, d % 2], S(4 + d % 2), ALU.mult)
                        ins.then_inc(y_read, 1)
                        if first:
                            dve.wait_ge(y_read, layer * per.y_read + 8 * first + d + 1)
                            ins = tt_(merged[:, d], merged[:, d], gy[:, d % 2], ALU.add)
                            if first == 2:
                                ins.then_inc(m_ready, 1)
                                if d:
                                    dve.wait_ge(m_hi, layer * per.m_hi + d)
                                    tt_(fLo[0][:, d - 1], merged[:, d - 1], fHi[0][:, d - 1].bitcast(F32), ALU.subtract).then_inc(m_lo, 1)
                    if first == 2:
                        dve.wait_ge(m_hi, layer * per.m_hi + 8)
                        tt_(fLo[0][:, 7], merged[:, 7], fHi[0][:, 7].bitcast(F32), ALU.subtract).then_inc(m_lo, 1)

                scale_x(0)
                norm_low(0)

                dve.wait_ge(x_stored, layer * per.x_stored + 16)
                nc.vector.memset(xrow[0:40], 0.0).then_inc(vector_step, 1)
                dve.wait_ge(vector_step, layer * per.vector_step + steps.next())
                dve.wait_ge(unit_done, layer * per.unit_done + UNIT_NO[("misc", 0)] + 1)
                b0 = bank_of(0)
                ts_(xrow[0:HEADS], b0[MISC_A:MISC_A + HEADS], p("dt", parts=HEADS), None, ALU.add)
                ts_(xrow[32:32 + HEADS], b0[MISC_B:MISC_B + HEADS], -1.0, None, ALU.mult)
                nc.vector.tensor_copy(krT[:], b0[MISC_ROPE:MISC_ROPE + ROPE]).then_inc(bank_read[TILE_NO[("misc", 0)] % 2], 1)
                for i in range(12):
                    name, j = ("k", "q", "v")[i // 4], i % 4
                    w0 = ({"q": 0, "k": 4, "v": 8}[name] + j) * CONV
                    dve.wait_ge(unit_done, layer * per.unit_done + UNIT_NO[(name, j)] + 1)
                    src, dst = bank_of(TILE_NO[(name, j)]), convd[:, i % 2]
                    if i >= 2:
                        dve.wait_ge(act_tile, layer * per.act_tile + i - 1)
                    ts_(dst, src, p("conv", w0 + 3), None, ALU.mult).then_inc(vector_step, 1)
                    dve.wait_ge(vector_step, layer * per.vector_step + steps.next())
                    for back in range(1, CONV):
                        ins = stt(dst[:, back:], src[:, 0:SEQ - back], p("conv", w0 + 3 - back), dst[:, back:], ALU.mult, ALU.add)
                        if back < CONV - 1:
                            ins.then_inc(vector_step, 1)
                            dve.wait_ge(vector_step, layer * per.vector_step + steps.next())
                    ins.then_inc(bank_read[TILE_NO[(name, j)] % 2], 1)
                    if i == 0:
                        stt(arow[0:40], xrow[0:40], -1.0, xrow[0:40], ALU.mult, ALU.max).then_inc(soft_abs, 1)
                dve.wait_ge(soft_ln, layer * per.soft_ln + 1)
                ins = stt(xrow[0:40], xrow[0:40], 0.0, arow[0:40], ALU.max, ALU.add)
                ins.then_inc(soft_done, 1)
                dve.wait_ge(soft_done, layer * per.soft_done + 1)
                ts_(arow[0:HEADS], xrow[0:HEADS], expa[:], -1.0, ALU.mult, ALU.mult).then_inc(vector_step, 1)
                dve.wait_ge(vector_step, layer * per.vector_step + steps.next())
                nc.vector.tensor_tensor_scan(gcum[:], c("reset", parts=HEADS), arow[0:HEADS], 0.0, ALU.mult, ALU.add).then_inc(cum_done, 1)
                dve.wait_ge(cum_done, layer * per.cum_done + 1)
                dve.wait_ge(ln_rows, layer * per.ln_rows + 1)
                stt(rowb[:], lnk[:], -0.5, gcum[:], ALU.mult, ALU.subtract)
                stt(rowc[:], lnq[:], -0.5, gcum[:], ALU.mult, ALU.add)
                stt(rowa[:], lnk[:], -0.5, gcum[:], ALU.mult, ALU.add).then_inc(vector_step, 1)
                dve.wait_ge(vector_step, layer * per.vector_step + steps.next())
                tt_(rowa[:], rowa[:], lnb[:], ALU.add).then_inc(vector_step, 1)
                dve.wait_ge(vector_step, layer * per.vector_step + steps.next())
                by_chunk = lambda r: r[:].rearrange("h (n t) -> h n t", t=CHUNK)
                tt_(by_chunk(rowe), by_chunk(rowb), by_chunk(gcum)[:, :, CHUNK - 1:CHUNK].broadcast_to([HEADS, CHUNKS, CHUNK]), ALU.add).then_inc(rows_done, 1)
                for j in range(PAIRS):
                    dve.wait_ge(qe_exp, layer * per.qe_exp + j + 1)
                    tt_(qeT[:, j], qT[:, j], decay[:, j % 2], ALU.mult).then_inc(qe_done, 1)
                nc.vector.memset(state[:], 0.0).then_inc(vector_step, 1)
                dve.wait_ge(vector_step, layer * per.vector_step + steps.next())

                def levels_mask(n):
                    return c("level", n, P).unsqueeze(1).broadcast_to([P, 8, P])

                def flat(t):
                    return t.rearrange("p a j n -> p (a j) n")

                for stage, tt, n in delta_schedule():
                    if stage == "prep":
                        by_head = lambda t: t.rearrange("p (h c) -> p h c", h=HEADS)
                        weight = lambda k: token[:, k, tt].unsqueeze(2).broadcast_to([P, HEADS, 64])
                        dve.wait_ge(tok_turned, layer * per.tok_turned + 2 * tt + 1)
                        tt_(by_head(rhsk[:]), by_head(S(0)), weight(0), ALU.mult)
                        tt_(by_head(kend[:, tt % 2]), by_head(S(0)), weight(1), ALU.mult).then_inc(tok_scaled, 1)
                        dve.wait_ge(tok_turned, layer * per.tok_turned + 2 * tt + 2)
                        tt_(by_head(rhsv[:]), by_head(S(1)), weight(2), ALU.mult).then_inc(tok_scaled, 1)
                    elif stage == "gram":
                        for i in range(4):
                            m = 4 * tt + i
                            dve.wait_ge(gram_done, layer * per.gram_done + m + 1)
                            dve.wait_ge(decay_done, layer * per.decay_done + m + 1)
                            dst = LT[:, i % 2] if i < 2 else intra[:, tt % 2, i % 2]
                            tt_(dst.rearrange("p j n -> p (j n)"), S(i % 2), decay[:, i % 2], ALU.mult).then_inc(gated_done, 1)
                    elif stage == "level" and n == 0:
                        dve.wait_ge(gated_done, layer * per.gated_done + 4 * tt + 2)
                        tt_(flat(CT[:]), flat(LT[:]), levels_mask(0), ALU.mult).then_inc(vector_step, 1)
                        dve.wait_ge(vector_step, layer * per.vector_step + steps.next())
                        tt_(flat(XT[:]), flat(CT[:]), c("ident").unsqueeze(1).broadcast_to([P, 8, P]), ALU.add).then_inc(xt_first, 1)
                        dve.wait_ge(xt_first, layer * per.xt_first + tt + 1)
                        tt_(flat(CT[:]), flat(LT[:]), levels_mask(1), ALU.mult).then_inc(ct_ready, 1)
                    elif stage == "level":
                        m = 10 * tt + 2 * (n - 1)
                        if n < 5:
                            dve.wait_ge(y_done, layer * per.y_done + m + 2)
                            tt_(flat(CT[:]), flat(LT[:]), levels_mask(n + 1), ALU.mult).then_inc(ct_ready, 1)
                        for hf in range(2):
                            dve.wait_ge(z_done, layer * per.z_done + m + hf + 1)
                            line = lambda t: t[:, hf].rearrange("p j n -> p (j n)")
                            ins = tt_(line(XT), line(XT), S(2), ALU.add)
                            if n < 5:
                                ins = tt_(line(X), line(X), S(3), ALU.add)
                            ins.then_inc(z_added, 1)
                    elif stage == "rec" and n in (0, 2):
                        m = 2 * tt + n // 2
                        hs = np.s_[32 * n:32 * n + 64]
                        if n == 0 and tt:
                            dve.wait_ge(o_done, layer * per.o_done + tt)
                        dve.wait_ge(ws_done, layer * per.ws_done + m + 1)
                        dve.wait_ge(sol_copied, layer * per.sol_copied + 2 * tt + 2)
                        tt_(vnew[hs], usol[hs, tt % 2], S(4)[hs], ALU.subtract).then_inc(vnew_done, 1)
                        if m:
                            dve.wait_ge(state_done, layer * per.state_done + m)
                        tt_(sdec[:], state[:], eglb[:, :, m:m + 1].broadcast_to([P, PAIRS, P]), ALU.mult).then_inc(vector_step, 1)
                        dve.wait_ge(vector_step, layer * per.vector_step + steps.next())
                    elif stage == "rec" and n in (1, 3):
                        m = 2 * tt + n // 2
                        dve.wait_ge(supd_done, layer * per.supd_done + m + 1)
                        upd = S(5).rearrange("p (j n) -> p j n", j=PAIRS)
                        tt_(state[0:64, :, 0:64], sdec[0:64, :, 0:64], upd[0:64, :, 0:64], ALU.add)
                        tt_(state[64:128, :, 64:128], sdec[64:128, :, 64:128], upd[64:128, :, 64:128], ALU.add).then_inc(state_done, 1)
                for j in range(4):
                    dve.wait_ge(oinv_ready, layer * per.oinv_ready + j + 1)
                    stt(vT[:, j], vT[:, j], p("onorm", 0), oinv[:, j % 2], ALU.mult, ALU.mult).then_inc(on_done, 1)
                for j in range(4):
                    n = TILE_NO[("z", j)]
                    dve.wait_ge(bank_read[n % 2], layer * per.bank_read + n // 2 + 1)
                    dve.wait_ge(on_done, layer * per.on_done + j + 1)
                    if j >= 2:
                        dve.wait_ge(b_lo, layer * per.b_lo + j - 1)
                    tt_(bval[:, j % 2], vT[:, j], szz[:, j % 2], ALU.mult).then_inc(bval_ready, 1)
                    if j:
                        dve.wait_ge(b_hi, layer * per.b_hi + j)
                        tt_(bLo[:, j - 1], bval[:, (j - 1) % 2], bHi[:, j - 1].bitcast(F32), ALU.subtract).then_inc(b_lo, 1)
                dve.wait_ge(b_hi, layer * per.b_hi + 4)
                tt_(bLo[:, 3], bval[:, 1], bHi[:, 3].bitcast(F32), ALU.subtract).then_inc(b_lo, 1)
                branch_merge(2, 0)

                for j in range(5):
                    dve.wait_ge(linv_ready, layer * per.linv_ready + (1 if j < 3 else 2))
                    if j >= 2:
                        dve.wait_ge(lat_lo, layer * per.lat_lo + j - 1)
                    g = p("qlat", j) if j < 3 else p("kvlat", j - 3)
                    stt(ltmp[:, j % 2], latT[:, j], g, linv[:, 0 if j < 3 else 1], ALU.mult, ALU.mult).then_inc(lat_val, 1)
                    if j:
                        dve.wait_ge(lat_hi, layer * per.lat_hi + j)
                        tt_(latLo[:, j - 1], ltmp[:, (j - 1) % 2], latHi[:, j - 1].bitcast(F32), ALU.subtract).then_inc(lat_lo, 1)
                dve.wait_ge(lat_hi, layer * per.lat_hi + 5)
                tt_(latLo[:, 4], ltmp[:, 0], latHi[:, 4].bitcast(F32), ALU.subtract).then_inc(lat_lo, 1)
                dve.wait_ge(kr_copied, layer * per.kr_copied + 1)
                dve.wait_ge(up_copied, layer * per.up_copied + 16)
                nc.vector.tensor_copy(ktm[:, :, :, NOPE:], krope[:].unsqueeze(2).broadcast_to([P, TT, HEADS, ROPE])).then_inc(kr_placed, 1)
                heads = lambda t: t[:].rearrange("p t h c -> p (t h) c")
                for n in range(2):
                    dve.wait_ge(qksq_ready, layer * per.qksq_ready + n + 1)
                    nc.vector.reduce_sum(headstat[:, n], heads(qksq), AX.X).then_inc(qkss_ready, 1)
                for n in range(2):
                    src = (qtm, ktm)[n]
                    dve.wait_ge(qkr_ready, layer * per.qkr_ready + n + 1)
                    tt_(heads(src), heads(src), headstat[:, n].unsqueeze(2).broadcast_to([P, TT * HEADS, QK]), ALU.mult).then_inc(vector_step, 1)
                    dve.wait_ge(vector_step, layer * per.vector_step + steps.next())
                    tt_(heads(src), heads(src), p("kg" if n else "qg").unsqueeze(1).broadcast_to([P, TT * HEADS, QK]), ALU.mult).then_inc(vector_step, 1)
                    dve.wait_ge(vector_step, layer * per.vector_step + steps.next())
                    x1, x2 = src[:, :, :, NOPE:NOPE + 16], src[:, :, :, NOPE + 16:]
                    sine, cosine = (trig[:, i].unsqueeze(2).broadcast_to([P, TT, HEADS, 16]) for i in range(2))
                    tt_(rtmp[:, 0], x1, cosine, ALU.mult)
                    tt_(rtmp[:, 1], x2, sine, ALU.mult)
                    tt_(rtmp[:, 2], x1, sine, ALU.mult)
                    tt_(rtmp[:, 3], x2, cosine, ALU.mult).then_inc(vector_step, 1)
                    dve.wait_ge(vector_step, layer * per.vector_step + steps.next())
                    tt_(x1, rtmp[:, 0], rtmp[:, 1], ALU.subtract)
                    ins = tt_(x2, rtmp[:, 2], rtmp[:, 3], ALU.add)
                    ins.then_inc(qk_ready, 1)
                for n in range(1, 16, 2):
                    dve.wait_ge(qk_turned, layer * per.qk_turned + n + 1)
                    nc.vector.tensor_copy((qhT, khT)[n // 8][0:QK, n % 8], S(n % 4)[0:QK]).then_inc(qk_copied_v, 1)

                def row_max(n):
                    dve.wait_ge(score_done, layer * per.score_done + n + 1)
                    if n >= 2:
                        dve.wait_ge(prob_done, layer * per.prob_done + n - 1)
                    w = (n // 8 + 1) * P
                    nc.vector.tensor_reduce(negmax[:, n % 2:n % 2 + 1], S(n % 2)[:, 0:w], AX.X, ALU.max, negate=True).then_inc(max_done, 1)

                def copy_turned(n):
                    w = (n // 8 + 1) * P
                    dve.wait_ge(pT_done, layer * per.pT_done + n + 1)
                    if n >= 2:
                        dve.wait_ge(pv_done, layer * per.pv_done + n - 1)
                    nc.vector.tensor_copy(probT[:, n % 2, 0:w], S(2 + n % 2)[:, 0:w]).then_inc(pT_copied, 1)

                def normalise(i):
                    dve.wait_ge(pv_done, layer * per.pv_done + 8 * i + 8)
                    nc.vector.reciprocal(pinv[:], psums[:, i % 2]).then_inc(vector_step, 1)
                    dve.wait_ge(vector_step, layer * per.vector_step + steps.next())
                    if i >= 2:
                        dve.wait_ge(o_turned, layer * per.o_turned + i - 1)
                    tt_(otm[:, i % 2].rearrange("p (h c) -> p h c", h=HEADS), S(4 + i % 2).rearrange("p (h c) -> p h c", h=HEADS),
                                          pinv[:].unsqueeze(2).broadcast_to([P, HEADS, 64]), ALU.mult).then_inc(otm_ready, 1)

                def outputs_low(i):
                    dve.wait_ge(b_hi, layer * per.b_hi + 4 + i + 1)
                    tt_(bLo[:, :, i * P:(i + 1) * P], bank_of(i).rearrange("p (j n) -> p j n", j=4), bHi[:, :, i * P:(i + 1) * P].bitcast(F32), ALU.subtract).then_inc(b_lo, 1)

                for n in range(32 + 1):
                    if n < 32:
                        row_max(n)
                    if n >= 1:
                        copy_turned(n - 1)
                    if n % 8 == 2 and n > 8:
                        normalise(n // 8 - 1)
                    if n % 8 == 6 and n > 8:
                        outputs_low(n // 8 - 1)
                normalise(3)
                outputs_low(3)
                branch_merge(1, 1)

                tt_(p("wsp").rearrange("p (g n) -> p g n", g=8), p("wsp").rearrange("p (g n) -> p g n", g=8),
                                       c("tril").unsqueeze(1).broadcast_to([P, 8, P]), ALU.mult).then_inc(wsp_masked, 1)
                dve.wait_ge(ainv_ready, layer * per.ainv_ready + 1)
                for j in range(4):
                    stt(avT[:, j], avT[:, j], p("sgu", j), ainv[:], ALU.mult, ALU.mult).then_inc(av_scaled, 1)
                for t in range(TT):
                    dve.wait_ge(av_turned, layer * per.av_turned + t + 1)
                    nc.vector.tensor_copy(vtok[:, t], S(t % 2)).then_inc(vtok_ready, 1)
                for j in range(4):
                    dve.wait_ge(sv_done, layer * per.sv_done + j + 1)
                    if j >= 2:
                        dve.wait_ge(b_lo, layer * per.b_lo + 8 + j - 1)
                    tt_(aval[:, j % 2], auT[:, j], S(2 + j % 2), ALU.mult).then_inc(bval_ready, 1)
                    if j:
                        dve.wait_ge(b_hi, layer * per.b_hi + 8 + j)
                        tt_(bLo[:, j - 1], aval[:, (j - 1) % 2], bHi[:, j - 1].bitcast(F32), ALU.subtract).then_inc(b_lo, 1)
                dve.wait_ge(b_hi, layer * per.b_hi + 12)
                tt_(bLo[:, 3], aval[:, 1], bHi[:, 3].bitcast(F32), ALU.subtract).then_inc(b_lo, 1)
                branch_merge(0, 2)

                dve.wait_ge(x_loaded, layer * per.x_loaded + 16)
                for half in range(2):
                    dve.wait_ge(unit_done, layer * per.unit_done + UNIT_NO[("out", 4 * half + 3)] + 1)
                    for t in range(TT):
                        o = xs[:, t, half * 512:half * 512 + 512]
                        tt_(o, o, ps[:, (2 + 4 * half + t) % 8], ALU.add).then_inc(x_added, 1)
                scale_x(1)
                norm_low(1)
                with dve.Fori(0, 2) as q2:
                    for b in range(2):
                        q = q2 * 2 + b
                        for n in range(8):
                            dve.wait_ge(f_hi, layer * per.f_hi + q * 8 + (n + 1))
                            nc.vector.tensor_tensor(fsq[:, n % 2], relu[:, n % 2], relu[:, n % 2], ALU.mult).then_inc(fsq_step, 1)
                            dve.wait_ge(fsq_step, layer * per.fsq_step + q * 8 + (n + 1))
                            tt_(fLo[b][:, n], fsq[:, n % 2], fHi[b][:, n].bitcast(F32), ALU.subtract).then_inc(f_lo, 1)
                        for half in range(2):
                            dve.wait_ge(unit_done, layer * per.unit_done + q * 16 + (FF0 + 8 + 4 * half + 4))
                            for t in range(TT):
                                o = xs[:, t, half * 512:half * 512 + 512]
                                tt_(o, o, S((4 * half + t) % 6), ALU.add).then_inc(x_added, 1)
                assert steps.n == VECTOR_STEPS or not VECTOR_STEPS, ("VECTOR_STEPS", steps.n)


def shape_constants():
    t = np.zeros((P, NCST), np.float32)

    def put(name, a):
        a = np.asarray(a, np.float32)
        t[:a.shape[0], CST[name][0]:CST[name][0] + a.reshape(a.shape[0], -1).shape[1]] = a.reshape(a.shape[0], -1)

    i, m = np.arange(P)[:, None], np.arange(P)[None, :]
    same = (i // CHUNK) == (m // CHUNK)
    put("ident", i == m)
    put("incl", np.where(same & (i <= m), 0.0, NEG))
    put("strict", np.where(same & (i < m), 0.0, NEG))
    put("level", np.stack([np.where((i // (2 * s) == m // (2 * s)) & (i // s % 2 == 0) & (m // s % 2 == 1), -1.0, 0.0)
                           for s in (1, 2, 4, 8, 16, 32)], 1))
    h8, h = np.arange(HEADS)[:, None, None], np.arange(HEADS)[None, :, None]
    put("sel", np.broadcast_to(h8 == h, (HEADS, HEADS, P)))
    j = np.arange(PAIRS)[None, :, None]
    put("pair", h8 == 2 * j + np.arange(P)[None, None, :] // 64)
    put("ind", np.arange(8)[None, None, :] == 2 * j + np.arange(P)[:, None, None] // 64)
    put("block", same)
    put("ones", np.ones((P, P)))
    put("reset", np.broadcast_to(np.arange(SEQ)[None] % CHUNK != 0, (P, SEQ)))
    put("causal", np.where(m <= i, 0.0, NEG))
    put("tril", m <= i)
    half = ROPE // 2
    freq = (np.float32(1) / (np.float32(ROPE_BASE) ** (np.arange(half, dtype=np.float32) / np.float32(half)))).astype(np.float32)
    put("freq", np.broadcast_to(freq, (P, half)))
    return t


def lay_out_weights(w_in, w_q_up, w_kv_up, w_branch, w_out, w_ff1, w_ff2):
    stream = np.zeros((DEPTH * U, P, UCOLS), np.float32)
    at_col = {"q": C_Q, "k": C_K, "v": C_V, "z": C_Z, "lat": Q_LAT, "av": A_V, "au": A_U}

    def tiles(w, k0, nk, c0, n):
        return w[k0 * P:(k0 + nk) * P, c0:c0 + n].reshape(nk, P, n).transpose(1, 0, 2)

    for l in range(DEPTH):
        for u, (kind, i) in enumerate(UNITS):
            dst = stream[l * U + u]
            if kind == "misc":
                v = dst.reshape(P, KD, P)
                v[:, :, MISC_ROPE:MISC_ROPE + ROPE] = tiles(w_in[l], 0, KD, K_ROPE, ROPE)
                v[:, :, MISC_B:MISC_B + HEADS] = tiles(w_in[l], 0, KD, C_B, HEADS)
                v[:, :, MISC_A:MISC_A + HEADS] = tiles(w_in[l], 0, KD, C_A, HEADS)
                continue
            if kind in at_col:
                t = tiles(w_in[l], 0, KD, at_col[kind] + i * P, P)
            elif kind.startswith("gate"):
                t = tiles(w_in[l], 0, KD, GATES + int(kind[4]) * D + i * P, P)
            elif kind == "qup":
                t = tiles(w_q_up[l], 0, 3, i * 192, 192)
            elif kind == "kvup":
                t = tiles(w_kv_up[l], 0, 2, i * 512, 512)
            elif kind[0] == "y":
                t = tiles(w_branch[l, int(kind[1])], 0, 4, i * 256, 256)
            elif kind == "out":
                t = tiles(w_out[l], 2 * (i % 4), 2, i // 4 * 512, 512)
            elif kind == "ff1":
                t = tiles(w_ff1[l], 0, KD, i * P, P)
            else:
                q, n = divmod(i, 8)
                t = tiles(w_ff2[l], 8 * q + 2 * (n % 4), 2, n // 4 * 512, 512)
            dst[:, :t.shape[1] * t.shape[2]] = t.reshape(P, -1)
    return stream


def lay_out_params(norm1_g, sgu_norm_g, w_spatial, b_spatial, q_lat_norm_g, kv_lat_norm_g, q_norm_g, k_norm_g,
                   conv_w, a_log, dt_bias, o_norm_g, norm2_g):
    t = np.zeros((DEPTH + 1, P, NPRM), np.float32)

    def put(l, name, a):
        t[l, :a.shape[0], PRM[name][0]:PRM[name][0] + a.shape[1]] = a

    for l in range(DEPTH + 1):
        src = min(l, DEPTH - 1)
        columns = lambda v: v.reshape(-1, P).T
        put(l, "g1", columns(norm1_g[src]))
        put(l, "g2", columns(norm2_g[src]))
        put(l, "sgu", columns(sgu_norm_g[src]))
        put(l, "qlat", columns(q_lat_norm_g[src]))
        put(l, "kvlat", columns(kv_lat_norm_g[src]))
        put(l, "onorm", np.concatenate([o_norm_g[src], o_norm_g[src]])[:, None])
        put(l, "conv", conv_w[src].reshape(CONV, 12, P).transpose(2, 1, 0).reshape(P, -1))
        put(l, "qg", np.broadcast_to(q_norm_g[src], (P, QK)))
        put(l, "kg", np.broadcast_to(k_norm_g[src], (P, QK)))
        put(l, "alog", a_log[src][:, None])
        put(l, "dt", dt_bias[src][:, None])
        put(l, "bsp", b_spatial[src])
        put(l, "wsp", w_spatial[src].transpose(1, 0, 2).reshape(P, -1))
    return t


def kernel(x, positions, norm1_g, w_in, sgu_norm_g, w_spatial, b_spatial, q_lat_norm_g, w_q_up,
           kv_lat_norm_g, w_kv_up, q_norm_g, k_norm_g, conv_w, a_log, dt_bias, o_norm_g,
           w_branch, w_out, norm2_g, w_ff1, w_ff2):
    import concourse.bacc as bacc
    from concourse.bass_utils import run_bass_kernel_spmd

    a = lambda v: np.asarray(v)
    arrays = {
        "stream": lay_out_weights(*map(a, (w_in, w_q_up, w_kv_up, w_branch, w_out, w_ff1, w_ff2))),
        "params": lay_out_params(*map(a, (norm1_g, sgu_norm_g, w_spatial, b_spatial, q_lat_norm_g, kv_lat_norm_g,
                                          q_norm_g, k_norm_g, conv_w, a_log, dt_bias, o_norm_g, norm2_g))),
        "x": np.ascontiguousarray(a(x)[0]),
        "positions": np.ascontiguousarray(a(positions)[0].reshape(TT, P).T),
        "constants": shape_constants(),
    }
    nc = bacc.Bacc("TRN2", target_bir_lowering=False, num_devices=1)
    args = [nc.dram_tensor(n, v.shape, mybir.dt.from_np(v.dtype), kind="ExternalInput").ap() for n, v in arrays.items()]
    out = nc.dram_tensor("out", (SEQ, D), F32, kind="ExternalOutput").ap()
    hybrid_trunk(nc, args[0], args[1], args[2], args[3], args[4], out)
    r = run_bass_kernel_spmd(nc, [arrays], core_ids=[0])
    return r.results[0]["out"].reshape(1, SEQ, D)
```

```python
from contextlib import ExitStack

import numpy as np

import concourse.bass as bass
from concourse import mybir

F32 = mybir.dt.float32
F32R = mybir.dt.float32r
I32 = mybir.dt.int32
ALU = mybir.AluOpType
ACT = mybir.ActivationFunctionType
AX = mybir.AxisListType

P = 128
DEPTH = 2
SEQ = 512
D = 1024
TT = SEQ // P
KD = D // P
A_WIDTH, A_GROUPS = 512, 8
HEADS = 8
PAIRS = HEADS // 2
NOPE, ROPE, VDIM = 64, 32, 64
QK = NOPE + ROPE
Q_LORA, KV_LORA = 384, 256
CHUNK, CDIM = 64, 64
CHUNKS = SEQ // CHUNK
CONV = 4
FF = 4 * D
EPS = 1e-6
ROPE_BASE = 10000.0
NEG = -1.0e30

A_U, A_V = 0, 512
Q_LAT = 1024
KV_LAT = Q_LAT + Q_LORA
K_ROPE = KV_LAT + KV_LORA
C_Q = K_ROPE + ROPE
C_K, C_V = C_Q + 512, C_Q + 1024
C_Z = C_Q + 1536
C_B = C_Z + 512
C_A = C_B + HEADS
GATES = C_A + HEADS
D_IN = GATES + 3 * D

MISC_ROPE, MISC_B, MISC_A = 0, 32, 64

TILES = (
    [("misc", 0)]
    + [("k", j) for j in range(4)] + [("q", j) for j in range(4)] + [("v", j) for j in range(4)]
    + [("z", j) for j in range(4)] + [("gate2", d) for d in range(KD)]
    + [("lat", j) for j in range(5)] + [("av", j) for j in range(4)]
    + [("au", j) for j in range(4)] + [("gate1", d) for d in range(KD)]
    + [("gate0", d) for d in range(KD)]
)
TILE_NO = {t: n for n, t in enumerate(TILES)}


def unit_order():
    order = []
    for t in TILES:
        if t == ("av", 2):
            order += [("qup", c) for c in range(4)] + [("kvup", c) for c in range(2)]
        order.append(t)
        if t[0][:4] == "gate" and t[1] % 2 == 1:
            order.append(("y" + t[0][4], t[1] // 2))
    order += [("out", n) for n in range(8)]
    for q in range(4):
        order += [("ff1", 8 * q + n) for n in range(8)] + [("ff2", 8 * q + n) for n in range(8)]
    return order


UNITS = unit_order()
UNIT_NO = {u: n for n, u in enumerate(UNITS)}
U = len(UNITS)
UCOLS = 1024
RAW, RING = 2, 4
FF0 = UNIT_NO[("ff1", 0)]
assert U % RING == 0 and FF0 % RING == 0

CST = {}
_at = 0
for _name, _n in (("ident", P), ("incl", P), ("strict", P), ("level", 6 * P), ("pair", PAIRS * P),
                  ("ind", PAIRS * 8), ("block", P), ("ones", P), ("reset", SEQ), ("causal", P), ("tril", P),
                  ("freq", ROPE // 2), ("sel", HEADS * P)):
    CST[_name] = (_at, _at + _n)
    _at += _n
NCST = _at
NCST_F32 = CST["sel"][0]

LOW, STACK = 32, 32 + HEADS

PRM = {}
_at = 0
for _name, _n in (("g1", KD), ("g2", KD), ("sgu", 4), ("qlat", 3), ("kvlat", 2), ("onorm", 1), ("conv", 12 * CONV),
                  ("qg", ROPE), ("kg", ROPE), ("qgt", 1), ("kgt", 1), ("alog", 1), ("dt", 1), ("bsp", P), ("wsp", A_GROUPS * P)):
    PRM[_name] = (_at, _at + _n)
    _at += _n
NPRM = _at

VECTOR_STEPS = 71
SCALAR_STEPS = 11

ROUND = 1.5 * 2.0 ** 23
TWO_PI = (6.28125, 8117 * 2.0 ** -22, 2 * np.pi - 6.28125 - 8117 * 2.0 ** -22)
ROPE_STEPS = 16


class Steps:

    def __init__(self):
        self.n = 0

    def next(self):
        self.n += 1
        return self.n


class PerLayer:
    unit_split = U; unit_done = U
    x_stored = 32; prm_loaded = 16; x_loaded = 16
    stat_ready = 2; stat_summed = 2; rstd_ready = 2; xn_ready = 8; h_turned = 16; h_hi = 16; h_lo = 16
    act_tile = 12; csq_ready = 8; csq_summed = 8
    soft_abs = 1; soft_ln = 1; soft_done = 1; cum_done = 1; ln_rows = 1; rows_done = 1; rows_split = 2; egl_done = 1; rows_turned = 1; token_done = 1
    qe_bcast = 4; qe_exp = 4; qe_done = 4
    tok_turned = 8; tok_scaled = 8; expo_done = 16; decay_done = 16; gram_done = 16; gated_done = 16
    xt_first = 4; x_turned = 8; x_first = 8; ct_ready = 20; y_done = 40; y_copied = 40; z_done = 40; z_added = 40
    solved = 8; sol_copied = 8; ws_done = 8; inter_done = 8; vnew_done = 8; supd_done = 8; state_done = 8; o_done = 4; o_copied = 4
    osq_ready = 4; osq_summed = 4; oinv_ready = 4; on_done = 4
    bval_ready = 8; b_hi = 12; b_lo = 12
    y_read = 24; m_ready = 8; m_hi = 8; m_lo = 8
    lsq_ready = 5; lsq_step = 5; linv_ready = 2; lat_val = 5; lat_hi = 5; lat_lo = 5; kr_turned = 1; kr_copied = 1; kr_placed = 1
    up_done = 10; up_copied = 16; qksq_ready = 2; qkss_ready = 2; qkr_ready = 2; qk_ready = 2; qk_turned = 8; qk_copied_a = 6; qk_copied_v = 2
    score_done = 32; max_done = 32; prob_done = 32; pT_done = 32; pT_copied = 32; pv_done = 32; otm_ready = 4; o_turned = 4
    asq_ready = 4; asq_step = 4; ainv_ready = 1; au_ready = 4; av_scaled = 4; av_turned = 4; vtok_ready = 4
    wsp_masked = 1; wsp_turned = 2; wsp_copied = 2; sv_done = 4
    x_added = 40; f_hi = 32; f_lo = 32; fsq_step = 32
    vector_step = VECTOR_STEPS; scalar_step = SCALAR_STEPS
    bank_read = 27; hidden_read = 17


def delta_schedule():
    for tt in range(TT + 1):
        if tt < TT:
            yield "prep", tt, 0
            yield "gram", tt, 0
        for n in range(6):
            if tt < TT:
                yield "level", tt, n
            if tt > 0 and n < 5:
                yield "rec", tt - 1, n
        if tt < TT:
            yield "solve", tt, 0


def hybrid_trunk(nc, stream, params, x, positions, constants, out):
    with ExitStack() as ctx:
        def sb(name, shape, dt=F32):
            return ctx.enter_context(nc.sbuf_tensor(name, shape, dt))

        def sem(name):
            return ctx.enter_context(nc.semaphore(name))

        hHi, hLo = sb("hHi", [P, KD, SEQ], F32R), sb("hLo", [P, KD, SEQ], F32R)
        wraw = sb("wraw", [P, RAW, UCOLS])
        wHi, wLo = sb("wHi", [P, RING, UCOLS], F32R), sb("wLo", [P, RING, UCOLS], F32R)
        cst, prm = sb("cst", [P, NCST_F32]), sb("prm", [P, NPRM])
        identr, maskr = sb("identr", [P, P], F32R), sb("maskr", [P, 3, P], F32R)
        selr, pairr = sb("selr", [STACK, HEADS, P], F32R), sb("pairr", [STACK, PAIRS, P], F32R)
        posi, posf = sb("posi", [P, TT], I32), sb("posf", [P, TT])
        trig = sb("trig", [P, 2, TT, ROPE // 2])
        warm = sb("warm", [P, 1])
        epsb, epsb64, lnscale = sb("epsb", [P, 1]), sb("epsb64", [P, 1]), sb("lnscale", [P, 1])
        stat, rstd = sb("stat", [P, 2, TT]), sb("rstd", [P, TT])
        token = sb("token", [P, 3, TT, HEADS])
        eglb, egl, expa = sb("eglb", [P, PAIRS, CHUNKS]), sb("egl", [HEADS, CHUNKS]), sb("expa", [HEADS, 1])
        headstat = sb("headstat", [P, 2, TT * HEADS])
        negmax, psums, pinv = sb("negmax", [P, 2]), sb("psums", [P, 2, HEADS]), sb("pinv", [P, HEADS])

        def at(kib, name, shape, dt=F32):
            with ExitStack() as below:
                if kib:
                    below.enter_context(nc.sbuf_tensor(f"below_{name}", [P, kib * 256], F32))
                return below.enter_context(nc.sbuf_tensor(name, shape, dt))

        tile2 = [P, 2, SEQ]
        selin = at(32, "selin", [STACK, HEADS * P])
        xs, merged = at(0, "xs", [P, TT, D]), at(16, "merged", [P, KD, SEQ])
        bHi, bLo = at(32, "bHi", [P, 4, SEQ], F32R), at(40, "bLo", [P, 4, SEQ], F32R)
        sg, gy = at(96, "sg", tile2), at(100, "gy", tile2)
        kT, qT = at(0, "kT", [P, PAIRS, SEQ]), at(8, "qT", [P, PAIRS, SEQ])
        vT, qeT = at(16, "vT", [P, PAIRS, SEQ]), at(24, "qeT", [P, PAIRS, SEQ])
        convd, csq = at(40, "convd", tile2), at(44, "csq", tile2)
        rhsk, rhsv, kend = at(32, "rhsk", [P, 512]), at(34, "rhsv", [P, 512]), at(36, "kend", [P, 2, 512])
        unit8 = [P, 2, PAIRS, P]
        LT, X, XT = at(40, "LT", unit8), at(44, "X", unit8), at(48, "XT", unit8)
        Y, CT = at(52, "Y", unit8), at(56, "CT", unit8)
        intra, usol = at(60, "intra", [P, 2, 2, PAIRS, P]), at(68, "usol", [P, 2, 512])
        wsol, vnew = at(72, "wsol", [P, 2, PAIRS, P]), at(76, "vnew", [P, 512])
        state, sdec = at(78, "state", [P, PAIRS, P]), at(80, "sdec", [P, PAIRS, P])
        decay = at(82, "decay", tile2)
        xrow, arow = at(86, "xrow", [P, SEQ]), at(88, "arow", [P, SEQ])
        gcum, lnb = at(90, "gcum", [HEADS, SEQ]), at(92, "lnb", [HEADS, SEQ])
        rowa, rowb = at(94, "rowa", [HEADS, SEQ]), at(96, "rowb", [HEADS, SEQ])
        rowc, rowe = at(98, "rowc", [HEADS, SEQ]), at(100, "rowe", [HEADS, SEQ])
        lnk, lnq = at(102, "lnk", [HEADS, SEQ]), at(104, "lnq", [HEADS, SEQ])
        krT = at(106, "krT", [ROPE, SEQ])
        asplit, bsplit = at(86, "asplit", [STACK, SEQ], F32R), at(88, "bsplit", [STACK, SEQ], F32R)
        csplit = at(102, "csplit", [STACK, SEQ], F32R)
        osq, oinv, szz, bval = at(52, "osq", tile2), at(68, "oinv", [P, 4, SEQ]), at(60, "szz", tile2), at(64, "bval", tile2)
        latT, lsq, linv = at(48, "latT", [P, 5, SEQ]), at(58, "lsq", tile2), at(62, "linv", tile2)
        latHi, latLo = at(68, "latHi", [P, 5, SEQ], F32R), at(78, "latLo", [P, 5, SEQ], F32R)
        ltmp = at(90, "ltmp", tile2)
        qtm, ktm = at(0, "qtm", [P, TT, HEADS, QK]), at(48, "ktm", [P, TT, HEADS, QK])
        krope, vtm, qksq = at(108, "krope", [P, TT, ROPE]), at(88, "vtm", [P, TT, 512]), at(32, "qksq", [P, TT, HEADS, QK])
        rtmp = at(98, "rtmp", [P, 4, TT, HEADS, ROPE // 2])
        qhT, khT = at(68, "qhT", [P, HEADS, SEQ]), at(0, "khT", [P, HEADS, SEQ])
        prob, probT, otm = at(84, "prob", tile2), at(96, "probT", tile2), at(100, "otm", [P, 2, 512])
        avT, auT, vtok = at(60, "avT", [P, 4, SEQ]), at(48, "auT", [P, 4, SEQ]), at(68, "vtok", [P, TT, 512])
        biasr = at(88, "biasr", [STACK, P], F32R)
        wspT, asq, ainv, aval = at(56, "wspT", [P, 8, P]), at(76, "asq", tile2), at(80, "ainv", [P, SEQ]), at(82, "aval", tile2)
        xn = at(16, "xn", [P, TT, D])
        fHi = [at(64, "fHi0", [P, 8, SEQ], F32R), at(32, "fHi1", [P, 8, SEQ], F32R)]
        fLo = [at(80, "fLo0", [P, 8, SEQ], F32R), at(48, "fLo1", [P, 8, SEQ], F32R)]
        relu, fsq = at(96, "relu", tile2), at(100, "fsq", tile2)

        ps = ctx.enter_context(nc.psum_tensor("ps", [P, 8, 512], F32))

        def c(name, i=0, n=None, parts=P):
            a, b = CST[name]
            return cst[0:parts, a + i * (n or 0):(a + (i + 1) * n if n else b)]

        def p(name, i=None, parts=P):
            a, b = PRM[name]
            return prm[0:parts, a:b] if i is None else prm[0:parts, a + i:a + i + 1]

        ident = c("ident")

        consts_in, sel_in, x_in, consts_done = sem("consts_in"), sem("sel_in"), sem("x_in"), sem("consts_done")
        rope_step, trig_done = sem("rope_step"), sem("trig_done")
        raw_loaded = [sem(f"raw{slot}_loaded") for slot in range(RAW)]
        unit_high = sem("unit_high")
        split_begun = sem("split_begun")
        unit_split, unit_done = sem("unit_split"), sem("unit_done")
        x_stored, prm_loaded, x_loaded = sem("x_stored"), sem("prm_loaded"), sem("x_loaded")
        rstd_ready, xn_ready, h_turned, h_hi = sem("rstd_ready"), sem("xn_ready"), sem("h_turned"), sem("h_hi")
        h_lo, stat_ready, stat_summed = sem("h_lo"), sem("stat_ready"), sem("stat_summed")
        act_tile, csq_ready, csq_summed = sem("act_tile"), sem("csq_ready"), sem("csq_summed")
        soft_abs, soft_ln, soft_done, cum_done = sem("soft_abs"), sem("soft_ln"), sem("soft_done"), sem("cum_done")
        ln_rows, rows_done, egl_done, rows_turned = sem("ln_rows"), sem("rows_done"), sem("egl_done"), sem("rows_turned")
        token_done, rows_split = sem("token_done"), sem("rows_split")
        qe_bcast, qe_exp, qe_done = sem("qe_bcast"), sem("qe_exp"), sem("qe_done")
        tok_turned, tok_scaled, expo_done, decay_done = sem("tok_turned"), sem("tok_scaled"), sem("expo_done"), sem("decay_done")
        gram_done, gated_done = sem("gram_done"), sem("gated_done")
        xt_first, x_turned, x_first, ct_ready = sem("xt_first"), sem("x_turned"), sem("x_first"), sem("ct_ready")
        y_done, y_copied, z_done, z_added = sem("y_done"), sem("y_copied"), sem("z_done"), sem("z_added")
        solved, sol_copied, ws_done, inter_done = sem("solved"), sem("sol_copied"), sem("ws_done"), sem("inter_done")
        vnew_done, supd_done, state_done, o_done = sem("vnew_done"), sem("supd_done"), sem("state_done"), sem("o_done")
        o_copied = sem("o_copied")
        osq_ready, osq_summed, oinv_ready, on_done = sem("osq_ready"), sem("osq_summed"), sem("oinv_ready"), sem("on_done")
        bval_ready, b_hi, b_lo = sem("bval_ready"), sem("b_hi"), sem("b_lo")
        y_read, m_ready, m_hi, m_lo = sem("y_read"), sem("m_ready"), sem("m_hi"), sem("m_lo")
        lsq_ready, lsq_step, linv_ready, lat_val = sem("lsq_ready"), sem("lsq_step"), sem("linv_ready"), sem("lat_val")
        lat_hi, lat_lo, kr_turned, kr_copied = sem("lat_hi"), sem("lat_lo"), sem("kr_turned"), sem("kr_copied")
        kr_placed = sem("kr_placed")
        up_done, up_copied, qksq_ready, qkss_ready = sem("up_done"), sem("up_copied"), sem("qksq_ready"), sem("qkss_ready")
        qkr_ready, qk_ready, qk_turned, qk_copied_a = sem("qkr_ready"), sem("qk_ready"), sem("qk_turned"), sem("qk_copied_a")
        qk_copied_v = sem("qk_copied_v")
        score_done, max_done, prob_done, pT_done = sem("score_done"), sem("max_done"), sem("prob_done"), sem("pT_done")
        pT_copied, pv_done, otm_ready, o_turned = sem("pT_copied"), sem("pv_done"), sem("otm_ready"), sem("o_turned")
        asq_ready, asq_step, ainv_ready, av_scaled = sem("asq_ready"), sem("asq_step"), sem("ainv_ready"), sem("av_scaled")
        au_ready = sem("au_ready")
        av_turned, vtok_ready, wsp_masked, wsp_turned = sem("av_turned"), sem("vtok_ready"), sem("wsp_masked"), sem("wsp_turned")
        wsp_copied, sv_done = sem("wsp_copied"), sem("sv_done")
        x_added, f_hi, f_lo, fsq_step = sem("x_added"), sem("f_hi"), sem("f_lo"), sem("fsq_step")
        vector_step, scalar_step = sem("vector_step"), sem("scalar_step")
        bank_read, hidden_read = [sem(f"bank_read{bank}") for bank in range(2)], [sem(f"hidden_read{bank}") for bank in range(2)]
        per = PerLayer

        def half_blocks(row, n, which):
            return row.rearrange("p (b two s) -> p b two s", two=2, s=2 ** n)[:, :, which]

        def bank_of(n):
            return ps[:, n % 2]

        def output_bank(i):
            return bank_of(TILE_NO[("au", i)])

        block = ctx.enter_context(nc.Block())

        @block.sync
        def _(sp):
            def load_unit(n, slot):
                sp.dma_start(wraw[:, slot], stream[bass.ds(n, 1)].rearrange("a p n -> p (a n)")
                             ).then_inc(raw_loaded[slot], 16)

            sp.dma_start(xs[:], x.rearrange("(t p) d -> p t d", p=P)).then_inc(x_in, 16)
            for slot in range(RAW):
                load_unit(slot, slot)
            with sp.Fori(1, DEPTH * U // RAW) as turn:
                n = turn * RAW
                for slot in range(RAW):
                    sp.wait_ge(unit_split, n + slot - RAW + 1)
                    load_unit(n + slot, slot)

        @block.gpsimd
        def _(pool):
            def split(slot, loads, done_before):
                raw = slot % RAW
                pool.wait_ge(raw_loaded[raw], 16 * loads)
                pool.sem_inc(split_begun, 1)
                nc.gpsimd.tensor_scalar(wHi[:, slot], wraw[:, raw], 1.0, 0.0, ALU.mult, ALU.add).then_inc(unit_high, 1)
                pool.wait_ge(unit_high, done_before + 1)
                nc.gpsimd.tensor_tensor(wLo[:, slot], wraw[:, raw], wHi[:, slot].bitcast(F32),
                                        ALU.subtract).then_inc(unit_split, 1)

            for slot in range(RING):
                split(slot, slot // RAW + 1, slot)
            with pool.Fori(1, DEPTH * U // RING) as turn:
                n = turn * RING
                for slot in range(RING):
                    pool.wait_ge(unit_done, n + slot - RING + 1)
                    split(slot, turn * (RING // RAW) + (slot // RAW + 1), n + slot)

        @block.tensor
        def _(pe):
            pe.wait_ge(consts_in, 32)
            pe.wait_ge(consts_done, 1)
            with pe.Fori(0, DEPTH) as layer:
                mm = nc.tensor.matmul

                def S(n):
                    return ps[:, 2 + n]

                def passes(o, l, lc, r, rc, start, stop):
                    (lh, ll), (rh, rl) = l, r
                    mm(o, lh[lc], rh[rc], start=start, stop=False)
                    mm(o, lh[lc], rl[rc], start=False, stop=False)
                    return mm(o, ll[lc], rh[rc], start=False, stop=stop)

                def turn_norm(which):
                    for group in range(0, KD, 4):
                        for t in range(TT):
                            pe.wait_ge(xn_ready, layer * per.xn_ready + 4 * which + t + 1)
                            for k in range(group, group + 4):
                                if group and t == 0:
                                    pe.wait_ge(h_lo, layer * per.h_lo + 8 * which + k - 3)
                                turned = nc.tensor.transpose(S(k % 4)[:, t * P:(t + 1) * P], xn[:, t, k * P:(k + 1) * P], ident)
                                if t == TT - 1:
                                    turned.then_inc(h_turned, 1)

                def project(tile, steps=range(KD)):
                    n, u = TILE_NO[tile], UNIT_NO[tile]
                    if steps[0] == 0:
                        if n >= 2:
                            pe.wait_ge(bank_read[n % 2], layer * per.bank_read + n // 2)
                        pe.wait_ge(unit_split, layer * per.unit_split + u + 1)
                    slot = u % RING
                    for k in steps:
                        if n == 0:
                            pe.wait_ge(h_lo, layer * per.h_lo + k + 1)
                        last = passes(bank_of(n), (wHi, wLo), np.s_[:, slot, k * P:(k + 1) * P], (hHi, hLo), np.s_[:, k], k == 0, k == KD - 1)
                    if steps[-1] == KD - 1:
                        last.then_inc(unit_done, 1)

                def sum_squares(i):
                    pe.wait_ge(csq_ready, layer * per.csq_ready + i + 1)
                    mm(S(i // 4)[0:HEADS], c("ind", i % 4, 8), csq[:, i % 2], start=i % 4 == 0, stop=i % 4 == 3).then_inc(csq_summed, 1)

                def delta_rows():
                    pe.wait_ge(rows_done, layer * per.rows_done + 1)
                    pe.wait_ge(egl_done, layer * per.egl_done + 1)
                    for j in range(PAIRS):
                        last = mm(S(3)[:, j * 8:j * 8 + 8], c("pair", j, P, 8), egl[:], start=True, stop=True)
                    for kind, row in enumerate((rowa, rowe, lnb)):
                        for t in range(TT):
                            last = nc.tensor.transpose(S(2)[:, (kind * TT + t) * 8:(kind * TT + t) * 8 + 8],
                                                       row[:, t * P:(t + 1) * P], c("ident", parts=8)[:, 0:8])
                    last.then_inc(rows_turned, 1)
                    for j in range(PAIRS):
                        if j == 0:
                            pe.wait_ge(rows_split, layer * per.rows_split + 1)
                        if j >= 2:
                            pe.wait_ge(qe_exp, layer * per.qe_exp + j - 1)
                        mm(S(4 + j % 2), pairr[:, j], csplit[:], start=True, stop=True).then_inc(qe_bcast, 1)

                def prep(tt):
                    ts = np.s_[tt * P:(tt + 1) * P]
                    if tt == 0:
                        pe.wait_ge(token_done, layer * per.token_done + 1)
                        pe.wait_ge(act_tile, layer * per.act_tile + 12)
                    else:
                        pe.wait_ge(sol_copied, layer * per.sol_copied + 2 * tt)
                    for j in range(PAIRS):
                        last = nc.tensor.transpose(S(0)[:, j * P:(j + 1) * P], kT[:, j, ts], ident)
                    last.then_inc(tok_turned, 1)
                    for j in range(PAIRS):
                        last = nc.tensor.transpose(S(1)[:, j * P:(j + 1) * P], vT[:, j, ts], ident)
                    last.then_inc(tok_turned, 1)

                def gram(tt):
                    ts = np.s_[tt * P:(tt + 1) * P]
                    if tt == 0:
                        pe.wait_ge(rows_split, layer * per.rows_split + 2)
                    for n in range(4):
                        kind, par = n // 2, n % 2
                        half = np.s_[64 * par:64 * par + 64]
                        m = 4 * tt + n
                        if n >= 2:
                            pe.wait_ge(decay_done, layer * per.decay_done + m - 1)
                        e = S(2 + par)
                        mm(e, identr[:], maskr[:, kind:kind + 1, :].broadcast_to([P, PAIRS, P]), start=True, stop=False)
                        for j in range(PAIRS):
                            h = 2 * j + par
                            o = e[:, j * P:(j + 1) * P]
                            mm(o, selr[:, h], (asplit, csplit)[kind][:, ts], start=False, stop=False)
                            last = mm(o, bsplit[:, ts], selr[:, h], start=False, stop=j == 3)
                        last.then_inc(expo_done, 1)
                        if n < 2:
                            pe.wait_ge(tok_scaled, layer * per.tok_scaled + 2 * tt + 1 + par)
                        else:
                            pe.wait_ge(gated_done, layer * per.gated_done + m - 1)
                        for j in range(PAIRS):
                            last = mm(S(par)[:, j * P:(j + 1) * P], kT[half, j, ts], (kT, qT)[kind][half, j, ts], start=True, stop=True)
                        last.then_inc(gram_done, 1)

                def level(tt, n):
                    if n == 0:
                        pe.wait_ge(xt_first, layer * per.xt_first + tt + 1)
                        pe.wait_ge(gated_done, layer * per.gated_done + 4 * tt + 4)
                        for hf in range(2):
                            for j in range(PAIRS):
                                last = nc.tensor.transpose(S(hf)[:, j * P:(j + 1) * P], XT[:, hf, j], ident)
                            last.then_inc(x_turned, 1)
                        return
                    m = 10 * tt + 2 * (n - 1)
                    pe.wait_ge(ct_ready, layer * per.ct_ready + 5 * tt + n)
                    for hf in range(2):
                        if n == 1:
                            pe.wait_ge(x_first, layer * per.x_first + 2 * tt + hf + 1)
                        else:
                            pe.wait_ge(z_added, layer * per.z_added + m + hf - 1)
                        for j in range(PAIRS):
                            last = mm(S(hf)[:, j * P:(j + 1) * P], CT[:, hf, j], X[:, hf, j], start=True, stop=True)
                        last.then_inc(y_done, 1)
                    for hf in range(2):
                        pe.wait_ge(y_copied, layer * per.y_copied + m + hf + 1)
                        for j in range(PAIRS):
                            last = mm(S(2 + hf)[:, j * 64:j * 64 + 64], Y[:, hf, j], half_blocks(XT[:, hf, j], n, 1), start=True, stop=True)
                        if n < 5:
                            for j in range(PAIRS):
                                last = mm(S(2 + hf)[:, 256 + j * 64:256 + j * 64 + 64], XT[:, hf, j], half_blocks(Y[:, hf, j], n, 0),
                                          start=True, stop=True)
                        last.then_inc(z_done, 1)

                def solve(tt):
                    pe.wait_ge(z_added, layer * per.z_added + 10 * tt + 10)
                    for h in range(HEADS):
                        last = mm(S(0)[:, h * 64:h * 64 + 64], XT[:, h % 2, h // 2], rhsv[:, h * 64:h * 64 + 64], start=True, stop=True)
                    last.then_inc(solved, 1)
                    for h in range(HEADS):
                        last = mm(S(1)[64 * (h % 2):64 * (h % 2) + 64, h // 2 * P:(h // 2 + 1) * P],
                                  rhsk[:, h * 64:h * 64 + 64], XT[:, h % 2, h // 2], start=True, stop=True)
                    last.then_inc(solved, 1)

                def recur(tt, part):
                    half = part // 2
                    hs = np.s_[64 * half:64 * half + 64]
                    m = 2 * tt + half
                    if part in (0, 2):
                        if part == 0:
                            pe.wait_ge(sol_copied, layer * per.sol_copied + 2 * tt + 2)
                            if tt:
                                pe.wait_ge(o_copied, layer * per.o_copied + tt)
                        if m:
                            pe.wait_ge(state_done, layer * per.state_done + m)
                        for j in range(PAIRS):
                            last = mm(S(4)[hs, j * P:(j + 1) * P], wsol[:, tt % 2, j, hs], state[:, j], start=True, stop=True)
                        last.then_inc(ws_done, 1)
                        for j in range(PAIRS):
                            t0 = j * P + 64 * half
                            last = mm(bank_of(0)[:, t0:t0 + 64], state[:, j], qeT[:, j, tt * P + 64 * half:tt * P + 64 * half + 64],
                                      start=part == 0 and j == 0, stop=False, skip_group_check=True)
                        last.then_inc(inter_done, 1)
                    elif part in (1, 3):
                        pe.wait_ge(vnew_done, layer * per.vnew_done + m + 1)
                        for j in range(PAIRS):
                            last = mm(S(5)[:, j * P:(j + 1) * P], kend[hs, tt % 2, j * P:(j + 1) * P], vnew[hs, j * P:(j + 1) * P],
                                      start=True, stop=True)
                        last.then_inc(supd_done, 1)
                    else:
                        for h in range(HEADS):
                            last = mm(bank_of(0)[64 * (h % 2):64 * (h % 2) + 64, h // 2 * P:(h // 2 + 1) * P],
                                      vnew[:, h * 64:h * 64 + 64], intra[:, tt % 2, h % 2, h // 2], start=False, stop=h == 7,
                                      skip_group_check=True)
                        last.then_inc(o_done, 1)

                def branch_out(br, first):
                    for d2 in range(4):
                        project((f"gate{br}", 2 * d2))
                        project((f"gate{br}", 2 * d2 + 1))
                        if d2 == 0:
                            pe.wait_ge(b_lo, layer * per.b_lo + 4 * first + 4)
                        u = UNIT_NO[(f"y{br}", d2)]
                        slot = u % RING
                        pe.wait_ge(unit_split, layer * per.unit_split + u + 1)
                        for i in range(2):
                            n = 8 * first + 2 * d2 + i
                            if n >= 2:
                                pe.wait_ge(y_read, layer * per.y_read + n - 1)
                            for k in range(4):
                                last = passes(S(4 + i), (wHi, wLo), np.s_[:, slot, k * 256 + i * P:k * 256 + (i + 1) * P],
                                              (bHi, bLo), np.s_[:, k], k == 0, k == 3)
                        last.then_inc(unit_done, 1)

                turn_norm(0)

                project(("misc", 0))
                for i in range(12):
                    project((("k", "q", "v")[i // 4], i % 4))
                    if 2 <= i < 10:
                        sum_squares(i - 2)
                project(("z", 0))
                delta_rows()
                for stage, tt, n in delta_schedule():
                    if stage == "prep":
                        prep(tt)
                    elif stage == "gram":
                        gram(tt)
                    elif stage == "level":
                        level(tt, n)
                    elif stage == "solve":
                        solve(tt)
                    else:
                        recur(tt, n)
                pe.wait_ge(o_copied, layer * per.o_copied + 4)
                project(("z", 1))
                for j in range(4):
                    pe.wait_ge(osq_ready, layer * per.osq_ready + j + 1)
                    mm(S(j), c("block"), osq[:, j % 2], start=True, stop=True).then_inc(osq_summed, 1)
                for j in range(2, 4):
                    project(("z", j))
                branch_out(2, 0)

                for j in range(5):
                    project(("lat", j))
                for j in range(5):
                    pe.wait_ge(lsq_ready, layer * per.lsq_ready + j + 1)
                    last = mm(S(0 if j < 3 else 1), c("ones"), lsq[:, j % 2], start=j in (0, 3), stop=j in (2, 4))
                    last.then_inc(lsq_step, 1)
                for t in range(TT):
                    last = nc.tensor.transpose(S(2)[:, t * ROPE:(t + 1) * ROPE], krT[:, t * P:(t + 1) * P], c("ident", parts=ROPE)[:, 0:ROPE])
                last.then_inc(kr_turned, 1)
                project(("av", 0))
                project(("av", 1))
                for n in range(6):
                    u = UNIT_NO[("qup", n)] if n < 4 else UNIT_NO[("kvup", n - 4)]
                    k0, nk, w = (0, 3, 192) if n < 4 else (3, 2, 512)
                    slot = u % RING
                    pe.wait_ge(unit_split, layer * per.unit_split + u + 1)
                    pe.wait_ge(lat_lo, layer * per.lat_lo + k0 + nk)
                    for t in range(TT):
                        g = n * 2 + t // 2 if n < 4 else 8 + (n - 4) * 4 + t
                        if (n >= 4 or t % 2 == 0) and g >= 4:
                            pe.wait_ge(up_copied, layer * per.up_copied + g - 3)
                        if (n, t) in ((0, 2), (1, 0)):
                            pe.wait_ge(kr_copied, layer * per.kr_copied + 1)
                            pe.wait_ge(linv_ready, layer * per.linv_ready + 2)
                        o = S(g % 4)[:, (t % 2) * 192:(t % 2) * 192 + 192] if n < 4 else S(g % 4)
                        for k in range(nk):
                            last = passes(o, (latHi, latLo), np.s_[:, k0 + k, t * P:(t + 1) * P],
                                          (wHi, wLo), np.s_[:, slot, k * w:(k + 1) * w], k == 0, k == nk - 1)
                        if t == TT - 1:
                            last.then_inc(unit_done, 1)
                        elif n >= 4 or t % 2:
                            last.then_inc(up_done, 1)
                project(("av", 2))
                project(("av", 3))
                for m in range(8):
                    if m == 4:
                        project(("au", 0))
                    if m % 4 == 0:
                        pe.wait_ge(qk_ready, layer * per.qk_ready + m // 4 + 1)
                    if m == 7:
                        pe.wait_ge(qk_copied_v, layer * per.qk_copied_v + 1)
                    elif m >= 2:
                        pe.wait_ge(qk_copied_a, layer * per.qk_copied_a + m - 1)
                    for n in (2 * m, 2 * m + 1):
                        for t in range(TT):
                            last = nc.tensor.transpose(S(n % 4)[0:QK, t * P:(t + 1) * P], (qtm, ktm)[m // 4][:, t, n % 8], ident)
                    last.then_inc(qk_turned, 1)
                pe.wait_ge(qk_copied_a, layer * per.qk_copied_a + 6)
                pe.wait_ge(qk_copied_v, layer * per.qk_copied_v + 2)

                def scores(n):
                    i, h = n // 8, n % 8
                    w = (i + 1) * P
                    if n >= 2:
                        pe.wait_ge(prob_done, layer * per.prob_done + n - 1)
                    bank = S(n % 2)
                    mm(bank[:, 0:w], qhT[0:QK, h, i * P:w], khT[0:QK, h, 0:w], start=True, stop=False)
                    mm(bank[:, i * P:w], identr[:], maskr[:, 2], start=False, stop=True).then_inc(score_done, 1)

                def turn_probs(n):
                    pe.wait_ge(prob_done, layer * per.prob_done + n + 1)
                    if n >= 2:
                        pe.wait_ge(pT_copied, layer * per.pT_copied + n - 1)
                    for kb in range(n // 8 + 1):
                        last = nc.tensor.transpose(S(2 + n % 2)[:, kb * P:(kb + 1) * P], prob[:, n % 2, kb * P:(kb + 1) * P], ident)
                    last.then_inc(pT_done, 1)

                def weigh(n):
                    i, h = n // 8, n % 8
                    pe.wait_ge(pT_copied, layer * per.pT_copied + n + 1)
                    if h == 0 and i >= 2:
                        pe.wait_ge(otm_ready, layer * per.otm_ready + i - 1)
                    for kb in range(i + 1):
                        last = mm(S(4 + i % 2)[:, h * 64:h * 64 + 64], probT[:, n % 2, kb * P:(kb + 1) * P],
                                  vtm[:, kb, h * 64:h * 64 + 64], start=kb == 0, stop=kb == i)
                    last.then_inc(pv_done, 1)

                def turn_outputs(i):
                    pe.wait_ge(otm_ready, layer * per.otm_ready + i + 1)
                    n = TILE_NO[("au", i)]
                    pe.wait_ge(bank_read[n % 2], layer * per.bank_read + n // 2 + 1)
                    if i >= 2:
                        pe.wait_ge(b_lo, layer * per.b_lo + 4 + i - 1)
                    for j in range(4):
                        last = nc.tensor.transpose(output_bank(i)[:, j * P:(j + 1) * P], otm[:, i % 2, j * P:(j + 1) * P], ident)
                    last.then_inc(o_turned, 1)

                for n in range(32 + 2):
                    if n < 32:
                        scores(n)
                        if n in (16, 24):
                            pe.wait_ge(b_lo, layer * per.b_lo + 4 + n // 8 - 1)
                        if n >= 8:
                            project(("au", n // 8), range(n % 8, n % 8 + 1))
                    if 1 <= n <= 32:
                        turn_probs(n - 1)
                    if n >= 2:
                        weigh(n - 2)
                    if n % 8 == 4 and n > 8:
                        turn_outputs(n // 8 - 1)
                turn_outputs(3)

                for j in range(4):
                    pe.wait_ge(asq_ready, layer * per.asq_ready + j + 1)
                    mm(S(0), c("ones"), asq[:, j % 2], start=j == 0, stop=j == 3).then_inc(asq_step, 1)
                pe.wait_ge(wsp_masked, layer * per.wsp_masked + 1)
                for g in range(8):
                    last = nc.tensor.transpose(S(1 + g // 4)[:, g % 4 * P:(g % 4 + 1) * P], p("wsp")[:, g * P:(g + 1) * P], ident)
                    if g % 4 == 3:
                        last.then_inc(wsp_turned, 1)

                branch_out(1, 1)

                pe.wait_ge(av_scaled, layer * per.av_scaled + 4)
                pe.wait_ge(wsp_copied, layer * per.wsp_copied + 2)
                pe.wait_ge(ainv_ready, layer * per.ainv_ready + 1)
                for t in range(TT):
                    if t >= 2:
                        pe.wait_ge(vtok_ready, layer * per.vtok_ready + t - 1)
                    for j in range(4):
                        last = nc.tensor.transpose(S(t % 2)[:, j * P:(j + 1) * P], avT[:, j, t * P:(t + 1) * P], ident)
                    last.then_inc(av_turned, 1)
                pe.wait_ge(vtok_ready, layer * per.vtok_ready + 4)
                for j in range(4):
                    if j >= 2:
                        pe.wait_ge(bval_ready, layer * per.bval_ready + 4 + j - 1)
                    o = S(2 + j % 2)
                    mm(o, pairr[:, j], biasr[:].unsqueeze(1).broadcast_to([STACK, TT, P]), start=True, stop=False,
                       skip_group_check=True)
                    for t in range(TT):
                        for par in range(2):
                            g = 2 * j + par
                            last = mm(o[64 * par:64 * par + 64, t * P:(t + 1) * P], vtok[:, t, g * 64:g * 64 + 64], wspT[:, g],
                                      start=False, stop=t == 3, skip_group_check=True)
                    last.then_inc(sv_done, 1)
                branch_out(0, 2)

                for half in range(2):
                    for kk in range(4):
                        u = UNIT_NO[("out", 4 * half + kk)]
                        slot = u % RING
                        pe.wait_ge(unit_split, layer * per.unit_split + u + 1)
                        pe.wait_ge(m_lo, layer * per.m_lo + 2 * kk + 2)
                        if half and kk == 0:
                            pe.wait_ge(y_read, layer * per.y_read + 24)
                        for t in range(TT):
                            o = ps[:, (2 + 4 * half + t) % 8]
                            for i in range(2):
                                k = 2 * kk + i
                                last = passes(o, (fHi[0], fLo[0]), np.s_[:, k, t * P:(t + 1) * P],
                                              (wHi, wLo), np.s_[:, slot, i * 512:(i + 1) * 512], k == 0, k == 7)
                        last.then_inc(unit_done, 1)
                turn_norm(1)

                with pe.Fori(0, 2) as q2:
                    for b in range(2):
                        q = q2 * 2 + b
                        for f in range(8):
                            slot = f % RING
                            pe.wait_ge(hidden_read[f % 2], layer * per.hidden_read + q * 4 + f // 2 + 1)
                            pe.wait_ge(unit_split, layer * per.unit_split + q * 16 + (FF0 + f + 1))
                            for k in range(KD):
                                last = passes(bank_of(f), (wHi, wLo), np.s_[:, slot, k * P:(k + 1) * P], (hHi, hLo), np.s_[:, k], k == 0, k == KD - 1)
                            last.then_inc(unit_done, 1)
                        for half in range(2):
                            for kk in range(4):
                                slot = kk % RING
                                pe.wait_ge(unit_split, layer * per.unit_split + q * 16 + (FF0 + 8 + 4 * half + kk + 1))
                                if half == 0:
                                    pe.wait_ge(f_lo, layer * per.f_lo + q * 8 + (2 * kk + 2))
                                    if kk == 0:
                                        pe.wait_ge(x_added, layer * per.x_added + q * 8 + 8)
                                for t in range(TT):
                                    if half and kk == 0 and t >= 2:
                                        pe.wait_ge(x_added, layer * per.x_added + q * 8 + (8 + t - 1))
                                    o = S((4 * half + t) % 6)
                                    for i in range(2):
                                        k = 2 * kk + i
                                        last = passes(o, (fHi[b], fLo[b]), np.s_[:, k, t * P:(t + 1) * P],
                                                      (wHi, wLo), np.s_[:, slot, i * 512:(i + 1) * 512], k == 0, k == 7)
                                last.then_inc(unit_done, 1)

        @block.scalar
        def _(act):
            act.dma_start(cst[:], constants[:, 0:NCST_F32]).then_inc(consts_in, 16)
            act.dma_start(selin[:], constants[0:STACK, NCST_F32:NCST]).then_inc(sel_in, 16)
            act.dma_start(posi[:], positions).then_inc(consts_in, 16)
            act.dma_start(prm[:], params[0]).then_inc(prm_loaded, 16)
            act.wait_ge(consts_in, 32)
            act.wait_ge(sel_in, 16)
            nc.scalar.copy(selr[:].rearrange("p h n -> p (h n)"), selin[:])
            nc.scalar.copy(pairr[:].rearrange("p j n -> p (j n)"), c("pair", parts=STACK))
            nc.scalar.copy(identr[:], ident)
            nc.scalar.copy(maskr[:, 0], c("strict"))
            nc.scalar.copy(maskr[:, 1], c("incl"))
            nc.scalar.copy(maskr[:, 2], c("causal")).then_inc(consts_done, 1)

            def square(half, t):
                w = np.s_[half * 512:half * 512 + 512]
                return nc.scalar.activation(xn[:, t, w], xs[:, t, w], ACT.Square, accum_out=stat[:, half, t:t + 1])

            def store_x(half):
                w = np.s_[half * 512:half * 512 + 512]
                act.dma_start(out[:, w].rearrange("(t p) d -> p t d", p=P), xs[:, :, w]).then_inc(x_stored, 16)

            act.wait_ge(x_in, 16)
            for half in range(2):
                store_x(half)
                for tt in range(TT):
                    last = square(half, tt)
            last.then_inc(stat_ready, 1)
            act.wait_ge(rope_step, ROPE_STEPS)
            nc.scalar.activation(trig[:], trig[:], ACT.Sin).then_inc(trig_done, 1)
            with act.Fori(0, DEPTH) as layer:
                steps = Steps()
                f = nc.scalar.activation

                def S(n):
                    return ps[:, 2 + n]

                def norm_scales(which):
                    act.wait_ge(stat_summed, layer * per.stat_summed + which + 1)
                    f(rstd[:], stat[:, 0], ACT.Sqrt, bias=epsb[:], scale=1.0 / D).then_inc(rstd_ready, 1)

                def norm_high(which):
                    for k in range(KD):
                        act.wait_ge(h_turned, layer * per.h_turned + 8 * which + k + 1)
                        if k == 0 and which == 0:
                            act.wait_ge(prm_loaded, layer * per.prm_loaded + 16)
                        f(hHi[:, k], S(k % 4), ACT.Copy, scale=p("g2" if which else "g1", k)).then_inc(h_hi, 1)

                def inverse_root(o, i, scale):
                    f(o, i, ACT.Ln, bias=epsb[0:o.shape[0]], scale=scale).then_inc(scalar_step, 1)
                    act.wait_ge(scalar_step, layer * per.scalar_step + steps.next())
                    return f(o, o, ACT.Exp, scale=-0.5)

                def branch_gates(br, first):
                    for d in range(KD):
                        tile = (f"gate{br}", d)
                        act.wait_ge(unit_done, layer * per.unit_done + UNIT_NO[tile] + 1)
                        n = 8 * first + d
                        if n >= 2:
                            act.wait_ge(y_read, layer * per.y_read + n - 1)
                        f(sg[:, d % 2], bank_of(TILE_NO[tile]), ACT.Sigmoid).then_inc(bank_read[TILE_NO[tile] % 2], 1)
                        if first == 2 and d >= 1:
                            act.wait_ge(m_ready, layer * per.m_ready + d)
                            nc.scalar.copy(fHi[0][:, d - 1], merged[:, d - 1]).then_inc(m_hi, 1)
                    if first == 2:
                        act.wait_ge(m_ready, layer * per.m_ready + 8)
                        nc.scalar.copy(fHi[0][:, 7], merged[:, 7]).then_inc(m_hi, 1)

                norm_scales(0)
                norm_high(0)

                act.wait_ge(x_stored, layer * per.x_stored + 32)
                for i in range(12):
                    name, j = ("k", "q", "v")[i // 4], i % 4
                    n = TILE_NO[(name, j)]
                    act.wait_ge(bank_read[n % 2], layer * per.bank_read + n // 2 + 1)
                    dst = (kT, qT, vT)[i // 4][:, j]
                    f(dst, convd[:, i % 2], ACT.Silu).then_inc(act_tile, 1)
                    if i < 8:
                        act.wait_ge(act_tile, layer * per.act_tile + i + 1)
                        if i >= 2:
                            act.wait_ge(csq_summed, layer * per.csq_summed + i - 1)
                        f(csq[:, i % 2], dst, ACT.Square).then_inc(csq_ready, 1)
                    if i == 9:
                        act.wait_ge(soft_abs, layer * per.soft_abs + 1)
                        f(arow[0:40], arow[0:40], ACT.Exp, scale=-1.0).then_inc(scalar_step, 1)
                        act.wait_ge(scalar_step, layer * per.scalar_step + steps.next())
                        f(expa[:], p("alog", parts=HEADS), ACT.Exp).then_inc(scalar_step, 1)
                        act.wait_ge(scalar_step, layer * per.scalar_step + steps.next())
                        f(arow[0:40], arow[0:40], ACT.Ln, bias=1.0).then_inc(soft_ln, 1)
                        act.wait_ge(csq_summed, layer * per.csq_summed + 8)
                        f(lnk[:], S(0)[0:HEADS], ACT.Ln, bias=epsb[0:HEADS])
                        f(lnq[:], S(1)[0:HEADS], ACT.Ln, bias=epsb64[0:HEADS], scale=float(CDIM))
                    if i == 10:
                        act.wait_ge(soft_done, layer * per.soft_done + 1)
                        f(lnb[:], xrow[32:40], ACT.Copy, scale=-1.0).then_inc(ln_rows, 1)
                        act.wait_ge(cum_done, layer * per.cum_done + 1)
                        f(egl[:], gcum[:].rearrange("h (n t) -> h n t", t=CHUNK)[:, :, CHUNK - 1], ACT.Exp).then_inc(egl_done, 1)
                act.wait_ge(rows_turned, layer * per.rows_turned + 1)
                nc.scalar.copy(eglb[:], S(3)[:, 0:PAIRS * CHUNKS].rearrange("p (j n) -> p j n", j=PAIRS))
                f(token[:], S(2)[:, 0:3 * TT * HEADS].rearrange("p (a t h) -> p a t h", a=3, t=TT), ACT.Exp).then_inc(token_done, 1)
                for j in range(PAIRS):
                    act.wait_ge(qe_bcast, layer * per.qe_bcast + j + 1)
                    if j >= 2:
                        act.wait_ge(qe_done, layer * per.qe_done + j - 1)
                    f(decay[:, j % 2], S(4 + j % 2), ACT.Exp).then_inc(qe_exp, 1)

                for stage, tt, n in delta_schedule():
                    if stage == "gram":
                        for i in range(4):
                            m = 4 * tt + i
                            act.wait_ge(expo_done, layer * per.expo_done + m + 1)
                            if m < 2:
                                act.wait_ge(qe_done, layer * per.qe_done + 4)
                            else:
                                act.wait_ge(gated_done, layer * per.gated_done + m - 1)
                            f(decay[:, i % 2], S(2 + i % 2), ACT.Exp).then_inc(decay_done, 1)
                    elif stage == "level" and n == 0:
                        for hf in range(2):
                            act.wait_ge(x_turned, layer * per.x_turned + 2 * tt + hf + 1)
                            nc.scalar.copy(X[:, hf].rearrange("p j n -> p (j n)"), S(hf)).then_inc(x_first, 1)
                    elif stage == "level":
                        for hf in range(2):
                            m = 10 * tt + 2 * (n - 1) + hf
                            act.wait_ge(y_done, layer * per.y_done + m + 1)
                            nc.scalar.copy(Y[:, hf].rearrange("p j n -> p (j n)"), S(hf)).then_inc(y_copied, 1)
                    elif stage == "solve":
                        act.wait_ge(solved, layer * per.solved + 2 * tt + 1)
                        nc.scalar.copy(usol[:, tt % 2], S(0)).then_inc(sol_copied, 1)
                        act.wait_ge(solved, layer * per.solved + 2 * tt + 2)
                        nc.scalar.copy(wsol[:, tt % 2].rearrange("p j n -> p (j n)"), S(1)).then_inc(sol_copied, 1)
                    elif stage == "rec" and n == 4:
                        act.wait_ge(o_done, layer * per.o_done + tt + 1)
                        nc.scalar.copy(vT[:, :, tt * P:(tt + 1) * P], bank_of(0).rearrange("p (j n) -> p j n", j=PAIRS)).then_inc(o_copied, 1)
                act.wait_ge(o_copied, layer * per.o_copied + 4)
                for j in range(4):
                    if j >= 2:
                        act.wait_ge(osq_summed, layer * per.osq_summed + j - 1)
                    f(osq[:, j % 2], vT[:, j], ACT.Square).then_inc(osq_ready, 1)
                    if j == 1:
                        act.wait_ge(unit_done, layer * per.unit_done + UNIT_NO[("z", 0)] + 1)
                        f(szz[:, 0], bank_of(TILE_NO[("z", 0)]), ACT.Silu).then_inc(bank_read[TILE_NO[("z", 0)] % 2], 1)
                for j in range(4):
                    act.wait_ge(osq_summed, layer * per.osq_summed + j + 1)
                    f(oinv[:, j], S(j), ACT.Ln, bias=epsb[:], scale=1.0 / VDIM).then_inc(scalar_step, 1)
                for j in range(4):
                    act.wait_ge(scalar_step, layer * per.scalar_step + steps.next())
                    f(oinv[:, j], oinv[:, j], ACT.Exp, scale=-0.5).then_inc(oinv_ready, 1)
                for j in range(4):
                    if j >= 1:
                        act.wait_ge(unit_done, layer * per.unit_done + UNIT_NO[("z", j)] + 1)
                        if j >= 2:
                            act.wait_ge(bval_ready, layer * per.bval_ready + j - 1)
                        f(szz[:, j % 2], bank_of(TILE_NO[("z", j)]), ACT.Silu).then_inc(bank_read[TILE_NO[("z", j)] % 2], 1)
                    if j >= 1:
                        act.wait_ge(bval_ready, layer * per.bval_ready + j)
                        nc.scalar.copy(bHi[:, j - 1], bval[:, (j - 1) % 2]).then_inc(b_hi, 1)
                act.wait_ge(bval_ready, layer * per.bval_ready + 4)
                nc.scalar.copy(bHi[:, 3], bval[:, 1]).then_inc(b_hi, 1)
                branch_gates(2, 0)

                def take_av(j):
                    n = TILE_NO[("av", j)]
                    act.wait_ge(unit_done, layer * per.unit_done + UNIT_NO[("av", j)] + 1)
                    f(avT[:, j], bank_of(n), ACT.Gelu).then_inc(bank_read[n % 2], 1)

                for j in range(5):
                    act.wait_ge(unit_done, layer * per.unit_done + UNIT_NO[("lat", j)] + 1)
                    n = TILE_NO[("lat", j)]
                    nc.scalar.copy(latT[:, j], bank_of(n)).then_inc(bank_read[TILE_NO[("lat", j)] % 2], 1)
                    act.wait_ge(bank_read[n % 2], layer * per.bank_read + n // 2 + 1)
                    if j >= 2:
                        act.wait_ge(lsq_step, layer * per.lsq_step + j - 1)
                    f(lsq[:, j % 2], latT[:, j], ACT.Square).then_inc(lsq_ready, 1)
                act.wait_ge(lsq_step, layer * per.lsq_step + 3)
                f(linv[:, 0], S(0), ACT.Ln, bias=epsb[:], scale=1.0 / Q_LORA).then_inc(scalar_step, 1)
                act.wait_ge(lsq_step, layer * per.lsq_step + 5)
                f(linv[:, 1], S(1), ACT.Ln, bias=epsb[:], scale=1.0 / KV_LORA).then_inc(scalar_step, 1)
                for n in range(2):
                    act.wait_ge(scalar_step, layer * per.scalar_step + steps.next())
                    f(linv[:, n], linv[:, n], ACT.Exp, scale=-0.5).then_inc(linv_ready, 1)
                for j in range(5):
                    act.wait_ge(lat_val, layer * per.lat_val + j + 1)
                    nc.scalar.copy(latHi[:, j], ltmp[:, j % 2]).then_inc(lat_hi, 1)
                take_av(0)
                take_av(1)
                act.wait_ge(kr_turned, layer * per.kr_turned + 1)
                nc.scalar.copy(krope[:], S(2)[:, 0:TT * ROPE].rearrange("p (t r) -> p t r", t=TT)).then_inc(kr_copied, 1)

                def heads_scale(n):
                    act.wait_ge(qkss_ready, layer * per.qkss_ready + n + 1)
                    f(headstat[:, n], headstat[:, n], ACT.Ln, bias=epsb[:], scale=1.0 / QK).then_inc(scalar_step, 1)
                    act.wait_ge(scalar_step, layer * per.scalar_step + steps.next())
                    f(headstat[:, n], headstat[:, n], ACT.Exp, scale=-0.5, bias=lnscale[:] if n == 0 else 0.0).then_inc(qkr_ready, 1)

                seen = 0
                for n in range(6):
                    for t in range(TT):
                        if n < 4 and t % 2 == 0:
                            continue
                        if t == TT - 1:
                            act.wait_ge(unit_done, layer * per.unit_done + UNIT_NO[("qup", n) if n < 4 else ("kvup", n - 4)] + 1)
                        else:
                            seen += 1
                            act.wait_ge(up_done, layer * per.up_done + seen)
                        if n < 4:
                            g = n * 2 + t // 2
                            src = S(g % 4)[:, 0:384].rearrange("p (t h c) -> p t h c", t=2, h=2)
                            ins = nc.scalar.copy(qtm[:, t - 1:t + 1, 2 * n:2 * n + 2], src)
                        else:
                            g = 8 + (n - 4) * 4 + t
                            src = S(g % 4).rearrange("p (h c) -> p h c", h=4)
                            h0 = 4 * (n - 4)
                            nc.scalar.copy(ktm[:, t, h0:h0 + 4, 0:NOPE], src[:, :, 0:NOPE])
                            ins = nc.scalar.copy(vtm[:, t, h0 * 64:h0 * 64 + 256].rearrange("p (h c) -> p h c", h=4), src[:, :, NOPE:])
                        ins.then_inc(up_copied, 1)
                    if n == 3:
                        act.wait_ge(up_copied, layer * per.up_copied + 8)
                        f(qksq[:], qtm[:], ACT.Square).then_inc(qksq_ready, 1)
                    if n == 4:
                        heads_scale(0)
                act.wait_ge(up_copied, layer * per.up_copied + 16)
                act.wait_ge(kr_placed, layer * per.kr_placed + 1)
                act.wait_ge(qkss_ready, layer * per.qkss_ready + 1)
                f(qksq[:], ktm[:], ACT.Square).then_inc(qksq_ready, 1)
                take_av(2)
                heads_scale(1)
                take_av(3)
                for m in (0, 1, 2, 3, 4, 6):
                    act.wait_ge(qk_turned, layer * per.qk_turned + m + 1)
                    f((qhT, khT)[m // 4][0:QK, 2 * m % 8:2 * m % 8 + 2], ps[0:QK, 2 + 2 * (m % 2):4 + 2 * (m % 2)], ACT.Copy,
                      scale=p("kgt" if m // 4 else "qgt", 0, QK)).then_inc(qk_copied_a, 1)

                def outputs_high(i):
                    act.wait_ge(o_turned, layer * per.o_turned + i + 1)
                    nc.scalar.copy(bHi[:, :, i * P:(i + 1) * P], output_bank(i).rearrange("p (j n) -> p j n", j=4)).then_inc(b_hi, 1)

                def take_au(j):
                    act.wait_ge(unit_done, layer * per.unit_done + UNIT_NO[("au", j)] + 1)
                    nc.scalar.copy(auT[:, j], bank_of(TILE_NO[("au", j)])).then_inc(bank_read[TILE_NO[("au", j)] % 2], 1)

                def square_av(j):
                    if j >= 2:
                        act.wait_ge(asq_step, layer * per.asq_step + j - 1)
                    f(asq[:, j % 2], avT[:, j], ACT.Square).then_inc(asq_ready, 1)

                for n in range(32):
                    w = (n // 8 + 1) * P
                    act.wait_ge(max_done, layer * per.max_done + n + 1)
                    if n >= 2:
                        act.wait_ge(pT_done, layer * per.pT_done + n - 1)
                    f(prob[:, n % 2, 0:w], S(n % 2)[:, 0:w], ACT.Exp, bias=negmax[:, n % 2:n % 2 + 1],
                                        accum_out=psums[:, n // 8 % 2, n % 8:n % 8 + 1]).then_inc(prob_done, 1)
                    if n % 8 == 1 and n > 8:
                        take_au(n // 8 - 1)
                    if n % 8 == 5 and n > 8:
                        outputs_high(n // 8 - 1)
                take_au(3)
                for j in range(2):
                    n = TILE_NO[("av", 2 + j)]
                    act.wait_ge(bank_read[n % 2], layer * per.bank_read + n // 2 + 1)
                    square_av(j)
                outputs_high(3)
                for j in range(2, 4):
                    square_av(j)
                act.wait_ge(asq_step, layer * per.asq_step + 4)
                inverse_root(ainv[:], S(0), 1.0 / A_WIDTH).then_inc(ainv_ready, 1)
                for g in range(2):
                    act.wait_ge(wsp_turned, layer * per.wsp_turned + g + 1)
                    nc.scalar.copy(wspT[:, 4 * g:4 * g + 4].rearrange("p g n -> p (g n)"), S(1 + g)).then_inc(wsp_copied, 1)
                act.wait_ge(score_done, layer * per.score_done + 32)
                act.wait_ge(x_stored, layer * per.x_stored + 32)
                act.dma_start(xs[:], out.rearrange("(t p) d -> p t d", p=P)).then_inc(x_loaded, 16)
                branch_gates(1, 1)

                for j in range(4):
                    if j < 2:
                        n = TILE_NO[("au", 2 + j)]
                        act.wait_ge(bank_read[n % 2], layer * per.bank_read + n // 2 + 1)
                    f(auT[:, j], auT[:, j], ACT.Gelu).then_inc(au_ready, 1)
                for j in range(4):
                    act.wait_ge(bval_ready, layer * per.bval_ready + 4 + j + 1)
                    nc.scalar.copy(bHi[:, j], aval[:, j % 2]).then_inc(b_hi, 1)
                branch_gates(0, 2)

                nc.scalar.activation(warm[:], epsb[:], ACT.Sqrt)
                for half in range(2):
                    for tt in range(TT):
                        if half or tt == 0:
                            act.wait_ge(x_added, layer * per.x_added + (4 * half + tt + 1 if half else 4))
                        last = square(half, tt)
                last.then_inc(stat_ready, 1)
                norm_scales(1)
                norm_high(1)
                act.wait_ge(h_lo, layer * per.h_lo + 16)
                act.sem_inc(hidden_read[0], 1)
                act.sem_inc(hidden_read[1], 1)
                with act.Fori(0, 2) as q2:
                    for b in range(2):
                        q = q2 * 2 + b
                        for n in range(8):
                            act.wait_ge(unit_done, layer * per.unit_done + q * 16 + (FF0 + n + 1))
                            if n >= 2:
                                act.wait_ge(f_lo, layer * per.f_lo + q * 8 + (n - 1))
                            f(relu[:, n % 2], bank_of(n), ACT.Relu).then_inc(hidden_read[n % 2], 1)
                            act.wait_ge(hidden_read[n % 2], layer * per.hidden_read + q * 4 + (n // 2 + 2))
                            if n == 0:
                                act.wait_ge(unit_done, layer * per.unit_done + q * 16 + (FF0 - 16))
                            f(fHi[b][:, n], relu[:, n % 2], ACT.Square).then_inc(f_hi, 1)
                for half in range(2):
                    for tt in range(TT):
                        if half or tt == 0:
                            act.wait_ge(x_added, layer * per.x_added + 32 + (4 * half + tt + 1 if half else 4))
                        last = square(half, tt)
                    store_x(half)
                last.then_inc(stat_ready, 1)
                act.dma_start(prm[:], params[bass.ds(layer + 1, 1)].rearrange("a p n -> p (a n)")).then_inc(prm_loaded, 16)
                assert steps.n == SCALAR_STEPS or not SCALAR_STEPS, ("SCALAR_STEPS", steps.n)
            act.wait_ge(x_stored, 32 * (DEPTH + 1))
            act.wait_ge(prm_loaded, 16 * (DEPTH + 1))

        @block.vector
        def _(dve):
            turns = Steps()
            nc.vector.memset(epsb[:], EPS)
            nc.vector.memset(epsb64[:], CDIM * EPS)
            nc.vector.memset(lnscale[:], float(np.log(QK ** -0.5)))
            dve.wait_ge(consts_in, 32)
            nc.vector.tensor_copy(posf[:], posi[:]).then_inc(rope_step, 1)
            dve.wait_ge(rope_step, turns.next())
            ang = [gy[:, n, 0:TT * 16].rearrange("p (t r) -> p t r", t=TT) for n in range(2)]
            cyc = sg[:, 0, 0:TT * 16].rearrange("p (t r) -> p t r", t=TT)
            for n in range(2):
                nc.vector.tensor_tensor(ang[n], posf[:].unsqueeze(2).broadcast_to([P, TT, 16]),
                                                   c("freq").unsqueeze(1).broadcast_to([P, TT, 16]), ALU.mult).then_inc(rope_step, 1)
                dve.wait_ge(rope_step, turns.next())
                nc.vector.tensor_scalar(cyc, ang[n], float(1 / (2 * np.pi)), 0.25 * n, ALU.mult, ALU.add).then_inc(rope_step, 1)
                dve.wait_ge(rope_step, turns.next())
                nc.vector.tensor_scalar(cyc, cyc, ROUND, -ROUND, ALU.add, ALU.add).then_inc(rope_step, 1)
                dve.wait_ge(rope_step, turns.next())
                for part in TWO_PI:
                    nc.vector.scalar_tensor_tensor(ang[n], cyc, -part, ang[n], ALU.mult, ALU.add).then_inc(rope_step, 1)
                    dve.wait_ge(rope_step, turns.next())
                if n:
                    nc.vector.tensor_scalar(ang[n], ang[n], float(np.pi / 2), None, ALU.add).then_inc(rope_step, 1)
                    dve.wait_ge(rope_step, turns.next())
                nc.vector.tensor_scalar(trig[:, n], ang[n], 3.1415925, -3.1415925, ALU.min, ALU.max).then_inc(rope_step, 1)
                dve.wait_ge(rope_step, turns.next())
            assert turns.n == ROPE_STEPS, turns.n
            with dve.Fori(0, DEPTH) as layer:
                steps = Steps()
                tt_, ts_, stt = nc.vector.tensor_tensor, nc.vector.tensor_scalar, nc.vector.scalar_tensor_tensor

                def S(n):
                    return ps[:, 2 + n]

                def scale_x(which):
                    dve.wait_ge(stat_ready, layer * per.stat_ready + which + 1)
                    tt_(stat[:, 0], stat[:, 0], stat[:, 1], ALU.add).then_inc(stat_summed, 1)
                    dve.wait_ge(rstd_ready, layer * per.rstd_ready + which + 1)
                    nc.vector.reciprocal(rstd[:], rstd[:]).then_inc(vector_step, 1)
                    dve.wait_ge(vector_step, layer * per.vector_step + steps.next())
                    for t in range(TT):
                        ts_(xn[:, t], xs[:, t], rstd[:, t:t + 1], None, ALU.mult).then_inc(xn_ready, 1)

                def norm_low(which):
                    for k in range(KD):
                        dve.wait_ge(h_hi, layer * per.h_hi + 8 * which + k + 1)
                        stt(hLo[:, k], S(k % 4), p("g2" if which else "g1", k), hHi[:, k].bitcast(F32), ALU.mult, ALU.subtract).then_inc(h_lo, 1)

                def branch_merge(br, first):
                    for d in range(KD):
                        n = TILE_NO[(f"gate{br}", d)]
                        dve.wait_ge(bank_read[n % 2], layer * per.bank_read + n // 2 + 1)
                        dve.wait_ge(unit_done, layer * per.unit_done + UNIT_NO[(f"y{br}", d // 2)] + 1)
                        dst = merged[:, d] if first == 0 else gy[:, d % 2]
                        ins = tt_(dst, sg[:, d % 2], S(4 + d % 2), ALU.mult)
                        ins.then_inc(y_read, 1)
                        if first:
                            dve.wait_ge(y_read, layer * per.y_read + 8 * first + d + 1)
                            ins = tt_(merged[:, d], merged[:, d], gy[:, d % 2], ALU.add)
                            if first == 2:
                                ins.then_inc(m_ready, 1)
                                if d:
                                    dve.wait_ge(m_hi, layer * per.m_hi + d)
                                    tt_(fLo[0][:, d - 1], merged[:, d - 1], fHi[0][:, d - 1].bitcast(F32), ALU.subtract).then_inc(m_lo, 1)
                    if first == 2:
                        dve.wait_ge(m_hi, layer * per.m_hi + 8)
                        tt_(fLo[0][:, 7], merged[:, 7], fHi[0][:, 7].bitcast(F32), ALU.subtract).then_inc(m_lo, 1)

                scale_x(0)
                norm_low(0)

                dve.wait_ge(x_stored, layer * per.x_stored + 32)
                nc.vector.memset(xrow[0:40], 0.0).then_inc(vector_step, 1)
                dve.wait_ge(vector_step, layer * per.vector_step + steps.next())
                dve.wait_ge(unit_done, layer * per.unit_done + UNIT_NO[("misc", 0)] + 1)
                b0 = bank_of(0)
                ts_(xrow[0:HEADS], b0[MISC_A:MISC_A + HEADS], p("dt", parts=HEADS), None, ALU.add)
                ts_(xrow[32:32 + HEADS], b0[MISC_B:MISC_B + HEADS], -1.0, None, ALU.mult)
                nc.vector.tensor_copy(krT[:], b0[MISC_ROPE:MISC_ROPE + ROPE]).then_inc(bank_read[TILE_NO[("misc", 0)] % 2], 1)
                for i in range(12):
                    name, j = ("k", "q", "v")[i // 4], i % 4
                    w0 = ({"q": 0, "k": 4, "v": 8}[name] + j) * CONV
                    dve.wait_ge(unit_done, layer * per.unit_done + UNIT_NO[(name, j)] + 1)
                    src, dst = bank_of(TILE_NO[(name, j)]), convd[:, i % 2]
                    if i >= 2:
                        dve.wait_ge(act_tile, layer * per.act_tile + i - 1)
                    ts_(dst, src, p("conv", w0 + 3), None, ALU.mult).then_inc(vector_step, 1)
                    dve.wait_ge(vector_step, layer * per.vector_step + steps.next())
                    for back in range(1, CONV):
                        ins = stt(dst[:, back:], src[:, 0:SEQ - back], p("conv", w0 + 3 - back), dst[:, back:], ALU.mult, ALU.add)
                        if back < CONV - 1:
                            ins.then_inc(vector_step, 1)
                            dve.wait_ge(vector_step, layer * per.vector_step + steps.next())
                    ins.then_inc(bank_read[TILE_NO[(name, j)] % 2], 1)
                    if i == 0:
                        stt(arow[0:40], xrow[0:40], -1.0, xrow[0:40], ALU.mult, ALU.max).then_inc(soft_abs, 1)
                    if i == 10:
                        dve.wait_ge(soft_ln, layer * per.soft_ln + 1)
                        ins = stt(xrow[0:40], xrow[0:40], 0.0, arow[0:40], ALU.max, ALU.add)
                        ins.then_inc(soft_done, 1)
                        dve.wait_ge(soft_done, layer * per.soft_done + 1)
                        ts_(arow[0:HEADS], xrow[0:HEADS], expa[:], -1.0, ALU.mult, ALU.mult).then_inc(vector_step, 1)
                        dve.wait_ge(vector_step, layer * per.vector_step + steps.next())
                        nc.vector.tensor_tensor_scan(gcum[:], c("reset", parts=HEADS), arow[0:HEADS], 0.0, ALU.mult, ALU.add).then_inc(cum_done, 1)
                        dve.wait_ge(cum_done, layer * per.cum_done + 1)
                        dve.wait_ge(ln_rows, layer * per.ln_rows + 1)
                        stt(rowb[:], lnk[:], -0.5, gcum[:], ALU.mult, ALU.subtract)
                        stt(rowc[:], lnq[:], -0.5, gcum[:], ALU.mult, ALU.add)
                        stt(rowa[:], lnk[:], -0.5, gcum[:], ALU.mult, ALU.add).then_inc(vector_step, 1)
                        dve.wait_ge(vector_step, layer * per.vector_step + steps.next())
                        tt_(rowa[:], rowa[:], lnb[:], ALU.add).then_inc(vector_step, 1)
                        dve.wait_ge(vector_step, layer * per.vector_step + steps.next())
                        by_chunk = lambda r: r[:].rearrange("h (n t) -> h n t", t=CHUNK)
                        tt_(by_chunk(rowe), by_chunk(rowb), by_chunk(gcum)[:, :, CHUNK - 1:CHUNK].broadcast_to([HEADS, CHUNKS, CHUNK]), ALU.add).then_inc(rows_done, 1)
                        nc.vector.memset(csplit[:].bitcast(F32), 0.0).then_inc(vector_step, 1)
                        dve.wait_ge(vector_step, layer * per.vector_step + steps.next())
                        nc.vector.tensor_copy(csplit[0:HEADS], rowc[:]).then_inc(vector_step, 1)
                        dve.wait_ge(vector_step, layer * per.vector_step + steps.next())
                        tt_(csplit[LOW:LOW + HEADS], rowc[:], csplit[0:HEADS].bitcast(F32), ALU.subtract).then_inc(rows_split, 1)
                nc.vector.memset(asplit[:].bitcast(F32), 0.0)
                nc.vector.memset(bsplit[:].bitcast(F32), 0.0).then_inc(vector_step, 1)
                dve.wait_ge(vector_step, layer * per.vector_step + steps.next())
                nc.vector.tensor_copy(asplit[0:HEADS], rowa[:])
                nc.vector.tensor_copy(bsplit[0:HEADS], rowb[:]).then_inc(vector_step, 1)
                dve.wait_ge(vector_step, layer * per.vector_step + steps.next())
                tt_(asplit[LOW:LOW + HEADS], rowa[:], asplit[0:HEADS].bitcast(F32), ALU.subtract)
                tt_(bsplit[LOW:LOW + HEADS], rowb[:], bsplit[0:HEADS].bitcast(F32), ALU.subtract).then_inc(rows_split, 1)
                for j in range(PAIRS):
                    dve.wait_ge(qe_exp, layer * per.qe_exp + j + 1)
                    tt_(qeT[:, j], qT[:, j], decay[:, j % 2], ALU.mult).then_inc(qe_done, 1)
                nc.vector.memset(state[:], 0.0).then_inc(vector_step, 1)
                dve.wait_ge(vector_step, layer * per.vector_step + steps.next())

                def levels_mask(n):
                    return c("level", n, P).unsqueeze(1).broadcast_to([P, 8, P])

                def flat(t):
                    return t.rearrange("p a j n -> p (a j) n")

                for stage, tt, n in delta_schedule():
                    if stage == "prep":
                        by_head = lambda t: t.rearrange("p (h c) -> p h c", h=HEADS)
                        weight = lambda k: token[:, k, tt].unsqueeze(2).broadcast_to([P, HEADS, 64])
                        dve.wait_ge(tok_turned, layer * per.tok_turned + 2 * tt + 1)
                        tt_(by_head(rhsk[:]), by_head(S(0)), weight(0), ALU.mult)
                        tt_(by_head(kend[:, tt % 2]), by_head(S(0)), weight(1), ALU.mult).then_inc(tok_scaled, 1)
                        dve.wait_ge(tok_turned, layer * per.tok_turned + 2 * tt + 2)
                        tt_(by_head(rhsv[:]), by_head(S(1)), weight(2), ALU.mult).then_inc(tok_scaled, 1)
                    elif stage == "gram":
                        for i in range(4):
                            m = 4 * tt + i
                            dve.wait_ge(gram_done, layer * per.gram_done + m + 1)
                            dve.wait_ge(decay_done, layer * per.decay_done + m + 1)
                            dst = LT[:, i % 2] if i < 2 else intra[:, tt % 2, i % 2]
                            tt_(dst.rearrange("p j n -> p (j n)"), S(i % 2), decay[:, i % 2], ALU.mult).then_inc(gated_done, 1)
                            if i == 1:
                                dve.wait_ge(gated_done, layer * per.gated_done + 4 * tt + 2)
                                tt_(flat(CT[:]), flat(LT[:]), levels_mask(0), ALU.mult).then_inc(vector_step, 1)
                                dve.wait_ge(vector_step, layer * per.vector_step + steps.next())
                                tt_(flat(XT[:]), flat(CT[:]), c("ident").unsqueeze(1).broadcast_to([P, 8, P]), ALU.add).then_inc(xt_first, 1)
                    elif stage == "level" and n == 0:
                        dve.wait_ge(xt_first, layer * per.xt_first + tt + 1)
                        tt_(flat(CT[:]), flat(LT[:]), levels_mask(1), ALU.mult).then_inc(ct_ready, 1)
                    elif stage == "level":
                        m = 10 * tt + 2 * (n - 1)
                        if n < 5:
                            dve.wait_ge(y_done, layer * per.y_done + m + 2)
                            tt_(flat(CT[:]), flat(LT[:]), levels_mask(n + 1), ALU.mult).then_inc(ct_ready, 1)
                        for hf in range(2):
                            dve.wait_ge(z_done, layer * per.z_done + m + hf + 1)
                            line = lambda t, which: half_blocks(t[:, hf].rearrange("p j n -> p (j n)"), n, which)
                            new = S(2 + hf).rearrange("p (a b s) -> p a b s", a=2, s=2 ** n)
                            ins = tt_(line(XT, 1), line(XT, 1), new[:, 0], ALU.add)
                            if n < 5:
                                ins = tt_(line(X, 0), line(X, 0), new[:, 1], ALU.add)
                            ins.then_inc(z_added, 1)
                    elif stage == "rec" and n in (0, 2):
                        m = 2 * tt + n // 2
                        hs = np.s_[32 * n:32 * n + 64]
                        if n == 0 and tt:
                            dve.wait_ge(o_done, layer * per.o_done + tt)
                        dve.wait_ge(ws_done, layer * per.ws_done + m + 1)
                        dve.wait_ge(sol_copied, layer * per.sol_copied + 2 * tt + 2)
                        tt_(vnew[hs], usol[hs, tt % 2], S(4)[hs], ALU.subtract).then_inc(vnew_done, 1)
                        if m:
                            dve.wait_ge(state_done, layer * per.state_done + m)
                        tt_(sdec[:], state[:], eglb[:, :, m:m + 1].broadcast_to([P, PAIRS, P]), ALU.mult).then_inc(vector_step, 1)
                        dve.wait_ge(vector_step, layer * per.vector_step + steps.next())
                    elif stage == "rec" and n in (1, 3):
                        m = 2 * tt + n // 2
                        dve.wait_ge(supd_done, layer * per.supd_done + m + 1)
                        upd = S(5).rearrange("p (j n) -> p j n", j=PAIRS)
                        tt_(state[0:64, :, 0:64], sdec[0:64, :, 0:64], upd[0:64, :, 0:64], ALU.add)
                        tt_(state[64:128, :, 64:128], sdec[64:128, :, 64:128], upd[64:128, :, 64:128], ALU.add).then_inc(state_done, 1)
                for j in range(4):
                    dve.wait_ge(oinv_ready, layer * per.oinv_ready + j + 1)
                    stt(vT[:, j], vT[:, j], p("onorm", 0), oinv[:, j], ALU.mult, ALU.mult).then_inc(on_done, 1)
                for j in range(4):
                    n = TILE_NO[("z", j)]
                    dve.wait_ge(bank_read[n % 2], layer * per.bank_read + n // 2 + 1)
                    dve.wait_ge(on_done, layer * per.on_done + j + 1)
                    if j >= 2:
                        dve.wait_ge(b_lo, layer * per.b_lo + j - 1)
                    tt_(bval[:, j % 2], vT[:, j], szz[:, j % 2], ALU.mult).then_inc(bval_ready, 1)
                    if j:
                        dve.wait_ge(b_hi, layer * per.b_hi + j)
                        tt_(bLo[:, j - 1], bval[:, (j - 1) % 2], bHi[:, j - 1].bitcast(F32), ALU.subtract).then_inc(b_lo, 1)
                dve.wait_ge(b_hi, layer * per.b_hi + 4)
                tt_(bLo[:, 3], bval[:, 1], bHi[:, 3].bitcast(F32), ALU.subtract).then_inc(b_lo, 1)
                branch_merge(2, 0)

                for j in range(5):
                    dve.wait_ge(linv_ready, layer * per.linv_ready + (1 if j < 3 else 2))
                    if j >= 2:
                        dve.wait_ge(lat_lo, layer * per.lat_lo + j - 1)
                    g = p("qlat", j) if j < 3 else p("kvlat", j - 3)
                    stt(ltmp[:, j % 2], latT[:, j], g, linv[:, 0 if j < 3 else 1], ALU.mult, ALU.mult).then_inc(lat_val, 1)
                    if j:
                        dve.wait_ge(lat_hi, layer * per.lat_hi + j)
                        tt_(latLo[:, j - 1], ltmp[:, (j - 1) % 2], latHi[:, j - 1].bitcast(F32), ALU.subtract).then_inc(lat_lo, 1)
                dve.wait_ge(lat_hi, layer * per.lat_hi + 5)
                tt_(latLo[:, 4], ltmp[:, 0], latHi[:, 4].bitcast(F32), ALU.subtract).then_inc(lat_lo, 1)
                dve.wait_ge(kr_copied, layer * per.kr_copied + 1)
                nc.vector.tensor_copy(ktm[:, :, :, NOPE:], krope[:].unsqueeze(2).broadcast_to([P, TT, HEADS, ROPE])).then_inc(kr_placed, 1)
                heads = lambda t: t[:].rearrange("p t h c -> p (t h) c")

                def sum_heads(n):
                    dve.wait_ge(qksq_ready, layer * per.qksq_ready + n + 1)
                    nc.vector.reduce_sum(headstat[:, n], heads(qksq), AX.X).then_inc(qkss_ready, 1)

                def scale_heads(n):
                    src = (qtm, ktm)[n]
                    dve.wait_ge(qkr_ready, layer * per.qkr_ready + n + 1)
                    tt_(heads(src), heads(src), headstat[:, n].unsqueeze(2).broadcast_to([P, TT * HEADS, QK]), ALU.mult).then_inc(vector_step, 1)
                    dve.wait_ge(vector_step, layer * per.vector_step + steps.next())
                    rope = heads(src)[:, :, NOPE:]
                    tt_(rope, rope, p("kg" if n else "qg").unsqueeze(1).broadcast_to([P, TT * HEADS, ROPE]), ALU.mult).then_inc(vector_step, 1)
                    dve.wait_ge(vector_step, layer * per.vector_step + steps.next())

                def rotate_heads(n):
                    src = (qtm, ktm)[n]
                    x1, x2 = src[:, :, :, NOPE:NOPE + 16], src[:, :, :, NOPE + 16:]
                    sine, cosine = (trig[:, i].unsqueeze(2).broadcast_to([P, TT, HEADS, 16]) for i in range(2))
                    tt_(rtmp[:, 0], x1, cosine, ALU.mult)
                    tt_(rtmp[:, 1], x2, sine, ALU.mult)
                    tt_(rtmp[:, 2], x1, sine, ALU.mult)
                    tt_(rtmp[:, 3], x2, cosine, ALU.mult).then_inc(vector_step, 1)
                    dve.wait_ge(vector_step, layer * per.vector_step + steps.next())
                    tt_(x1, rtmp[:, 0], rtmp[:, 1], ALU.subtract)
                    tt_(x2, rtmp[:, 2], rtmp[:, 3], ALU.add).then_inc(qk_ready, 1)

                sum_heads(0)
                scale_heads(0)
                dve.wait_ge(trig_done, 1)
                sum_heads(1)
                rotate_heads(0)
                scale_heads(1)
                rotate_heads(1)
                for m in (5, 7):
                    dve.wait_ge(qk_turned, layer * per.qk_turned + m + 1)
                    ts_(khT[0:QK, 2 * m % 8:2 * m % 8 + 2], ps[0:QK, 2 + 2 * (m % 2):4 + 2 * (m % 2)], p("kgt", 0, QK), None,
                        ALU.mult).then_inc(qk_copied_v, 1)

                def row_max(n):
                    dve.wait_ge(score_done, layer * per.score_done + n + 1)
                    if n >= 2:
                        dve.wait_ge(prob_done, layer * per.prob_done + n - 1)
                    w = (n // 8 + 1) * P
                    nc.vector.tensor_reduce(negmax[:, n % 2:n % 2 + 1], S(n % 2)[:, 0:w], AX.X, ALU.max, negate=True).then_inc(max_done, 1)

                def copy_turned(n):
                    w = (n // 8 + 1) * P
                    dve.wait_ge(pT_done, layer * per.pT_done + n + 1)
                    if n >= 2:
                        dve.wait_ge(pv_done, layer * per.pv_done + n - 1)
                    nc.vector.tensor_copy(probT[:, n % 2, 0:w], S(2 + n % 2)[:, 0:w]).then_inc(pT_copied, 1)

                def normalise(i):
                    dve.wait_ge(pv_done, layer * per.pv_done + 8 * i + 8)
                    nc.vector.reciprocal(pinv[:], psums[:, i % 2]).then_inc(vector_step, 1)
                    dve.wait_ge(vector_step, layer * per.vector_step + steps.next())
                    if i >= 2:
                        dve.wait_ge(o_turned, layer * per.o_turned + i - 1)
                    tt_(otm[:, i % 2].rearrange("p (h c) -> p h c", h=HEADS), S(4 + i % 2).rearrange("p (h c) -> p h c", h=HEADS),
                                          pinv[:].unsqueeze(2).broadcast_to([P, HEADS, 64]), ALU.mult).then_inc(otm_ready, 1)

                def outputs_low(i):
                    dve.wait_ge(b_hi, layer * per.b_hi + 4 + i + 1)
                    tt_(bLo[:, :, i * P:(i + 1) * P], output_bank(i).rearrange("p (j n) -> p j n", j=4), bHi[:, :, i * P:(i + 1) * P].bitcast(F32), ALU.subtract).then_inc(b_lo, 1)

                for n in range(32 + 1):
                    if n < 32:
                        row_max(n)
                    if n >= 1:
                        copy_turned(n - 1)
                    if n % 8 == 2 and n > 8:
                        normalise(n // 8 - 1)
                    if n % 8 == 6 and n > 8:
                        outputs_low(n // 8 - 1)
                normalise(3)
                outputs_low(3)
                tt_(p("wsp").rearrange("p (g n) -> p g n", g=8), p("wsp").rearrange("p (g n) -> p g n", g=8),
                                       c("tril").unsqueeze(1).broadcast_to([P, 8, P]), ALU.mult).then_inc(wsp_masked, 1)
                nc.vector.memset(biasr[:].bitcast(F32), 0.0).then_inc(vector_step, 1)
                dve.wait_ge(vector_step, layer * per.vector_step + steps.next())
                nc.vector.tensor_copy(biasr[0:HEADS], p("bsp", parts=HEADS)).then_inc(vector_step, 1)
                dve.wait_ge(vector_step, layer * per.vector_step + steps.next())
                tt_(biasr[LOW:LOW + HEADS], p("bsp", parts=HEADS), biasr[0:HEADS].bitcast(F32), ALU.subtract)
                dve.wait_ge(ainv_ready, layer * per.ainv_ready + 1)
                for j in range(4):
                    stt(avT[:, j], avT[:, j], p("sgu", j), ainv[:], ALU.mult, ALU.mult).then_inc(av_scaled, 1)
                branch_merge(1, 1)

                for t in range(TT):
                    dve.wait_ge(av_turned, layer * per.av_turned + t + 1)
                    nc.vector.tensor_copy(vtok[:, t], S(t % 2)).then_inc(vtok_ready, 1)
                for j in range(4):
                    dve.wait_ge(sv_done, layer * per.sv_done + j + 1)
                    dve.wait_ge(au_ready, layer * per.au_ready + j + 1)
                    if j >= 2:
                        dve.wait_ge(b_lo, layer * per.b_lo + 8 + j - 1)
                    tt_(aval[:, j % 2], auT[:, j], S(2 + j % 2), ALU.mult).then_inc(bval_ready, 1)
                    if j:
                        dve.wait_ge(b_hi, layer * per.b_hi + 8 + j)
                        tt_(bLo[:, j - 1], aval[:, (j - 1) % 2], bHi[:, j - 1].bitcast(F32), ALU.subtract).then_inc(b_lo, 1)
                dve.wait_ge(b_hi, layer * per.b_hi + 12)
                tt_(bLo[:, 3], aval[:, 1], bHi[:, 3].bitcast(F32), ALU.subtract).then_inc(b_lo, 1)
                branch_merge(0, 2)

                dve.wait_ge(x_loaded, layer * per.x_loaded + 16)
                for half in range(2):
                    dve.wait_ge(unit_done, layer * per.unit_done + UNIT_NO[("out", 4 * half + 3)] + 1)
                    for t in range(TT):
                        o = xs[:, t, half * 512:half * 512 + 512]
                        tt_(o, o, ps[:, (2 + 4 * half + t) % 8], ALU.add).then_inc(x_added, 1)
                scale_x(1)
                norm_low(1)
                with dve.Fori(0, 2) as q2:
                    for b in range(2):
                        q = q2 * 2 + b
                        for n in range(8):
                            dve.wait_ge(f_hi, layer * per.f_hi + q * 8 + (n + 1))
                            nc.vector.tensor_tensor(fsq[:, n % 2], relu[:, n % 2], relu[:, n % 2], ALU.mult).then_inc(fsq_step, 1)
                            dve.wait_ge(fsq_step, layer * per.fsq_step + q * 8 + (n + 1))
                            tt_(fLo[b][:, n], fsq[:, n % 2], fHi[b][:, n].bitcast(F32), ALU.subtract).then_inc(f_lo, 1)
                        for half in range(2):
                            dve.wait_ge(unit_done, layer * per.unit_done + q * 16 + (FF0 + 8 + 4 * half + 4))
                            for t in range(TT):
                                o = xs[:, t, half * 512:half * 512 + 512]
                                tt_(o, o, S((4 * half + t) % 6), ALU.add).then_inc(x_added, 1)
                assert steps.n == VECTOR_STEPS or not VECTOR_STEPS, ("VECTOR_STEPS", steps.n)


def shape_constants():
    t = np.zeros((P, NCST), np.float32)

    def put(name, a):
        a = np.asarray(a, np.float32)
        t[:a.shape[0], CST[name][0]:CST[name][0] + a.reshape(a.shape[0], -1).shape[1]] = a.reshape(a.shape[0], -1)

    i, m = np.arange(P)[:, None], np.arange(P)[None, :]
    same = (i // CHUNK) == (m // CHUNK)
    put("ident", i == m)
    put("incl", np.where(same & (i <= m), 0.0, NEG))
    put("strict", np.where(same & (i < m), 0.0, NEG))
    put("level", np.stack([np.where((i // (2 * s) == m // (2 * s)) & (i // s % 2 == 0) & (m // s % 2 == 1), -1.0, 0.0)
                           for s in (1, 2, 4, 8, 16, 32)], 1))
    h8, h = np.arange(HEADS)[:, None, None], np.arange(HEADS)[None, :, None]
    twice = lambda a: np.concatenate([a, np.zeros((LOW - HEADS,) + a.shape[1:], bool), a])
    put("sel", twice(np.broadcast_to(h8 == h, (HEADS, HEADS, P))))
    j = np.arange(PAIRS)[None, :, None]
    put("pair", twice(h8 == 2 * j + np.arange(P)[None, None, :] // 64))
    put("ind", np.arange(8)[None, None, :] == 2 * j + np.arange(P)[:, None, None] // 64)
    put("block", same)
    put("ones", np.ones((P, P)))
    put("reset", np.broadcast_to(np.arange(SEQ)[None] % CHUNK != 0, (P, SEQ)))
    put("causal", np.where(m <= i, 0.0, NEG))
    put("tril", m <= i)
    half = ROPE // 2
    freq = (np.float32(1) / (np.float32(ROPE_BASE) ** (np.arange(half, dtype=np.float32) / np.float32(half)))).astype(np.float32)
    put("freq", np.broadcast_to(freq, (P, half)))
    return t


def lay_out_weights(w_in, w_q_up, w_kv_up, w_branch, w_out, w_ff1, w_ff2):
    stream = np.zeros((DEPTH * U, P, UCOLS), np.float32)
    at_col = {"q": C_Q, "k": C_K, "v": C_V, "z": C_Z, "lat": Q_LAT, "av": A_V, "au": A_U}

    def tiles(w, k0, nk, c0, n):
        return w[k0 * P:(k0 + nk) * P, c0:c0 + n].reshape(nk, P, n).transpose(1, 0, 2)

    for l in range(DEPTH):
        for u, (kind, i) in enumerate(UNITS):
            dst = stream[l * U + u]
            if kind == "misc":
                v = dst.reshape(P, KD, P)
                v[:, :, MISC_ROPE:MISC_ROPE + ROPE] = tiles(w_in[l], 0, KD, K_ROPE, ROPE)
                v[:, :, MISC_B:MISC_B + HEADS] = tiles(w_in[l], 0, KD, C_B, HEADS)
                v[:, :, MISC_A:MISC_A + HEADS] = tiles(w_in[l], 0, KD, C_A, HEADS)
                continue
            if kind in at_col:
                t = tiles(w_in[l], 0, KD, at_col[kind] + i * P, P)
            elif kind.startswith("gate"):
                t = tiles(w_in[l], 0, KD, GATES + int(kind[4]) * D + i * P, P)
            elif kind == "qup":
                t = tiles(w_q_up[l], 0, 3, i * 192, 192)
            elif kind == "kvup":
                t = tiles(w_kv_up[l], 0, 2, i * 512, 512)
            elif kind[0] == "y":
                t = tiles(w_branch[l, int(kind[1])], 0, 4, i * 256, 256)
            elif kind == "out":
                t = tiles(w_out[l], 2 * (i % 4), 2, i // 4 * 512, 512)
            elif kind == "ff1":
                t = tiles(w_ff1[l], 0, KD, i * P, P)
            else:
                q, n = divmod(i, 8)
                t = tiles(w_ff2[l], 8 * q + 2 * (n % 4), 2, n // 4 * 512, 512)
            dst[:, :t.shape[1] * t.shape[2]] = t.reshape(P, -1)
    return stream


def lay_out_params(norm1_g, sgu_norm_g, w_spatial, b_spatial, q_lat_norm_g, kv_lat_norm_g, q_norm_g, k_norm_g,
                   conv_w, a_log, dt_bias, o_norm_g, norm2_g):
    t = np.zeros((DEPTH + 1, P, NPRM), np.float32)

    def put(l, name, a):
        t[l, :a.shape[0], PRM[name][0]:PRM[name][0] + a.shape[1]] = a

    for l in range(DEPTH + 1):
        src = min(l, DEPTH - 1)
        columns = lambda v: v.reshape(-1, P).T
        put(l, "g1", columns(norm1_g[src]))
        put(l, "g2", columns(norm2_g[src]))
        put(l, "sgu", columns(sgu_norm_g[src]))
        put(l, "qlat", columns(q_lat_norm_g[src]))
        put(l, "kvlat", columns(kv_lat_norm_g[src]))
        put(l, "onorm", np.concatenate([o_norm_g[src], o_norm_g[src]])[:, None])
        put(l, "conv", conv_w[src].reshape(CONV, 12, P).transpose(2, 1, 0).reshape(P, -1))
        for name, gain in (("qg", q_norm_g[src]), ("kg", k_norm_g[src])):
            put(l, name, np.broadcast_to(gain[NOPE:], (P, ROPE)))
            put(l, name + "t", np.concatenate([gain[:NOPE], np.ones(ROPE, np.float32)])[:, None])
        put(l, "alog", a_log[src][:, None])
        put(l, "dt", dt_bias[src][:, None])
        put(l, "bsp", b_spatial[src])
        put(l, "wsp", w_spatial[src].transpose(1, 0, 2).reshape(P, -1))
    return t


def kernel(x, positions, norm1_g, w_in, sgu_norm_g, w_spatial, b_spatial, q_lat_norm_g, w_q_up,
           kv_lat_norm_g, w_kv_up, q_norm_g, k_norm_g, conv_w, a_log, dt_bias, o_norm_g,
           w_branch, w_out, norm2_g, w_ff1, w_ff2):
    import concourse.bacc as bacc
    from concourse.bass_utils import run_bass_kernel_spmd

    a = lambda v: np.asarray(v)
    arrays = {
        "stream": lay_out_weights(*map(a, (w_in, w_q_up, w_kv_up, w_branch, w_out, w_ff1, w_ff2))),
        "params": lay_out_params(*map(a, (norm1_g, sgu_norm_g, w_spatial, b_spatial, q_lat_norm_g, kv_lat_norm_g,
                                          q_norm_g, k_norm_g, conv_w, a_log, dt_bias, o_norm_g, norm2_g))),
        "x": np.ascontiguousarray(a(x)[0]),
        "positions": np.ascontiguousarray(a(positions)[0].reshape(TT, P).T),
        "constants": shape_constants(),
    }
    nc = bacc.Bacc("TRN2", target_bir_lowering=False, num_devices=1)
    args = [nc.dram_tensor(n, v.shape, mybir.dt.from_np(v.dtype), kind="ExternalInput").ap() for n, v in arrays.items()]
    out = nc.dram_tensor("out", (SEQ, D), F32, kind="ExternalOutput").ap()
    hybrid_trunk(nc, args[0], args[1], args[2], args[3], args[4], out)
    r = run_bass_kernel_spmd(nc, [arrays], core_ids=[0])
    return r.results[0]["out"].reshape(1, SEQ, D)
```
